# Optimizing a Trainium2 kernel written in Bass

```python
import jax
import jax.numpy as jnp
from jax import lax
import numpy as np

D_MODEL = 1024
BATCH = 1
SEQ = 128
DEPTH = 4
DEC_BATCH = 1
DEC_SEQ = 256
PAST_LEN = 128

GRID_W = 64
N_MIXERS = 3
N_ATTN_LAYERS = (DEPTH + 2) // 3
N_CONV_LAYERS = (DEPTH + 1) // 3
N_HGRN_LAYERS = DEPTH // 3
N_MOD = 9
N_NORMS = 6
D_FF = 2816
FFN_RES = 0.5
ATTN_HEADS = 16
ATTN_KV_HEADS = 4
ATTN_GROUPS = ATTN_HEADS // ATTN_KV_HEADS
HEAD_DIM = 64
ATTN_DIM = ATTN_HEADS * HEAD_DIM
WINDOW = 128
BLOCK = 128
ATTN_SCALE = HEAD_DIM ** -0.5
ROPE_BASE = 10000.0
ROPE_PAIRS_PER_AXIS = HEAD_DIM // 4
CONV_WIDTH = 3
HGRN_HEADS = 8
HGRN_DK = 128
HGRN_DV = D_MODEL // HGRN_HEADS
HGRN_FD = HGRN_HEADS * HGRN_DK
CHUNK = 16
EPS = 1e-6

kernel_name = 'hybrid_diffusion_prefix_trunk_step'

def rmsnorm(x, g):
    xf = x.astype(jnp.float32)
    y = xf * lax.rsqrt(jnp.mean(xf * xf, axis=-1, keepdims=True) + EPS)
    return y.astype(x.dtype) * g

def modulate(x, shift, scale):
    return x * (1 + scale) + shift

def adaln(cond, w, b):
    m = jax.nn.silu(cond) @ w + b
    return [t[:, None, :] for t in jnp.split(m, N_MOD, axis=-1)]

def ffn_sublayer(x, shift, scale, gate, g_pre, g_post, w_in, w_out):
    h = modulate(rmsnorm(x, g_pre), shift, scale)
    a, b = jnp.split(h @ w_in, 2, axis=-1)
    h = (jax.nn.silu(a) * b) @ w_out
    return x + FFN_RES * gate * rmsnorm(h, g_post)

def axial_rope(L):
    rows = L // GRID_W
    row = jnp.repeat(jnp.arange(rows), GRID_W).astype(jnp.float32)
    col = jnp.tile(jnp.arange(GRID_W), rows).astype(jnp.float32)
    inv = ROPE_BASE ** (-jnp.arange(ROPE_PAIRS_PER_AXIS, dtype=jnp.float32) / ROPE_PAIRS_PER_AXIS)
    ang = jnp.concatenate([row[:, None] * inv, col[:, None] * inv], axis=-1)
    return jnp.cos(ang), jnp.sin(ang)

def apply_rope(x, cos, sin):
    x1, x2 = jnp.split(x, 2, axis=-1)
    c = cos[None, :, None, :]
    s = sin[None, :, None, :]
    return jnp.concatenate([x1 * c - x2 * s, x1 * s + x2 * c], axis=-1).astype(x.dtype)

def attn_project(h, w_qkv):
    B, L, _ = h.shape
    q, k, v = jnp.split(h @ w_qkv, [ATTN_DIM, ATTN_DIM + ATTN_KV_HEADS * HEAD_DIM], axis=-1)
    return (q.reshape(B, L, ATTN_HEADS, HEAD_DIM),
            k.reshape(B, L, ATTN_KV_HEADS, HEAD_DIM),
            v.reshape(B, L, ATTN_KV_HEADS, HEAD_DIM))

def sink_logits(sink, shape):
    s = sink.astype(jnp.float32).reshape(ATTN_KV_HEADS, ATTN_GROUPS)
    s = s.reshape((1,) * (len(shape) - 4) + (ATTN_KV_HEADS, ATTN_GROUPS, 1, 1))
    return jnp.broadcast_to(s, shape[:-1] + (1,))

def attn_context(h, w_qkv, w_o, sink):
    B, L, _ = h.shape
    q, k, v = attn_project(h, w_qkv)
    nqb = L // BLOCK
    qb = jnp.moveaxis(q.reshape(B, nqb, BLOCK, ATTN_KV_HEADS, ATTN_GROUPS, HEAD_DIM), 1, 0)

    def block(qi):
        s = jnp.einsum('bqkgd,bskd->bkgqs', qi, k).astype(jnp.float32) * ATTN_SCALE
        p = jax.nn.softmax(jnp.concatenate([s, sink_logits(sink, s.shape)], axis=-1), axis=-1)
        return jnp.einsum('bkgqs,bskd->bqkgd', p[..., :-1].astype(v.dtype), v)

    o = jnp.moveaxis(lax.map(block, qb), 0, 1).reshape(B, L, ATTN_DIM)
    return o @ w_o, k, v

def attn_latent(h, w_qkv, w_o, sink, k_ctx, v_ctx):
    B, L, _ = h.shape
    q, k, v = attn_project(h, w_qkv)
    cos, sin = axial_rope(L)
    q = apply_rope(q, cos, sin)
    k = apply_rope(k, cos, sin)
    nb = L // BLOCK
    qb = q.reshape(B, nb, BLOCK, ATTN_KV_HEADS, ATTN_GROUPS, HEAD_DIM)

    def band(t):
        tp = jnp.pad(t, ((0, 0), (BLOCK, BLOCK), (0, 0), (0, 0))).reshape(B, nb + 2, BLOCK, ATTN_KV_HEADS, HEAD_DIM)
        return jnp.concatenate([tp[:, :-2], tp[:, 1:-1], tp[:, 2:]], axis=2)

    kb, vb = band(k), band(v)
    n_band = 3 * BLOCK
    qi = jnp.arange(BLOCK)[:, None]
    u = jnp.arange(n_band)[None, :]
    in_window = jnp.abs(qi + BLOCK - u) <= WINDOW
    kpos = (jnp.arange(nb)[:, None] - 1) * BLOCK + jnp.arange(n_band)[None, :]
    in_range = (kpos >= 0) & (kpos < L)
    mask = in_window[None] & in_range[:, None, :]
    s_lat = jnp.einsum('bnqkgd,bnskd->bnkgqs', qb, kb).astype(jnp.float32) * ATTN_SCALE
    s_lat = jnp.where(mask[None, :, None, None], s_lat, -jnp.inf)
    s_ctx = jnp.einsum('bnqkgd,bskd->bnkgqs', qb, k_ctx).astype(jnp.float32) * ATTN_SCALE
    logits = jnp.concatenate([s_lat, s_ctx, sink_logits(sink, s_lat.shape)], axis=-1)
    p = jax.nn.softmax(logits, axis=-1).astype(v.dtype)
    o = (jnp.einsum('bnkgqs,bnskd->bnqkgd', p[..., :n_band], vb)
         + jnp.einsum('bnkgqs,bskd->bnqkgd', p[..., n_band:-1], v_ctx))
    return o.reshape(B, L, ATTN_DIM) @ w_o

def short_conv(h, w_in, cw, cb, w_out):
    L = h.shape[1]
    bg, cg, u = jnp.split(h @ w_in, 3, axis=-1)
    z = cg * u
    pad = CONV_WIDTH // 2
    zp = jnp.pad(z, ((0, 0), (pad, pad), (0, 0)))
    conv = cb + sum(zp[:, j:j + L] * cw[j] for j in range(CONV_WIDTH))
    return (bg * conv) @ w_out

def chunk_gla(q, k, v, logf, s0):
    B, L, H, _ = q.shape
    DV = v.shape[-1]
    n = L // CHUNK
    q, k, v, logf = (t.astype(jnp.float32).reshape(B, n, CHUNK, H, t.shape[-1]) for t in (q, k, v, logf))
    b = jnp.cumsum(logf, axis=2)
    tri = jnp.tril(jnp.ones((CHUNK, CHUNK), bool))
    diff = b[:, :, :, None] - b[:, :, None, :]
    decay = jnp.exp(jnp.where(tri[None, None, :, :, None, None], diff, -jnp.inf))
    scores = jnp.einsum('bnthd,bnshd,bntshd->bnhts', q, k, decay)
    o_intra = jnp.einsum('bnhts,bnshv->bnthv', scores, v)
    b_last = b[:, :, -1]
    kv = jnp.einsum('bnshd,bnshv->bnhdv', k * jnp.exp(b_last[:, :, None] - b), v)

    def step(S, xs):
        dec, kv_n = xs
        return dec[..., None] * S + kv_n, S

    S_fin, S_prev = lax.scan(step, s0.astype(jnp.float32),
                             (jnp.moveaxis(jnp.exp(b_last), 1, 0), jnp.moveaxis(kv, 1, 0)))
    S_prev = jnp.moveaxis(S_prev, 0, 1)
    o_inter = jnp.einsum('bnthd,bnhdv->bnthv', q * jnp.exp(b), S_prev)
    return (o_intra + o_inter).reshape(B, L, H, DV), S_fin

def hgrn_lower_bound(lb_param, li):
    p = jax.nn.softmax(lb_param.astype(jnp.float32), axis=0)
    return jnp.cumsum(p, axis=0)[li] - p[0]

def hgrn_mixer(h, w_in, lb_f, lb_b, norm_g, w_out, s0_f, s0_b):
    B, L, _ = h.shape
    zq, zi, zf, zb, zg = jnp.split(
        h @ w_in, [HGRN_FD, HGRN_FD + D_MODEL, 2 * HGRN_FD + D_MODEL, 3 * HGRN_FD + D_MODEL], axis=-1)
    heads = lambda t: t.reshape(B, L, HGRN_HEADS, -1)
    q = heads(jax.nn.silu(zq)) * HGRN_DK ** -0.5
    v = heads(zi)

    def gates(z, lb):
        lb = lb.reshape(HGRN_HEADS, HGRN_DK)
        f = lb + (1 - lb) * jax.nn.sigmoid(heads(z).astype(jnp.float32))
        return 1 - f, jnp.log(f)

    k_f, lf_f = gates(zf, lb_f)
    k_b, lf_b = gates(zb, lb_b)
    rev = lambda t: jnp.flip(t, axis=1)
    o_f, S_f = chunk_gla(q, k_f, v, lf_f, s0_f)
    o_b, S_b = chunk_gla(rev(q), rev(k_b), rev(v), rev(lf_b), s0_b)
    o = o_f + rev(o_b)
    o = rmsnorm(o, norm_g) * jax.nn.silu(heads(zg))
    return o.reshape(B, L, D_MODEL).astype(h.dtype) @ w_out, S_f.astype(h.dtype), S_b.astype(h.dtype)

def setup_inputs(seed: int = 0) -> dict:
    key = jax.random.key(seed)
    ks = jax.random.split(key, 24)
    nrm = lambda k, shape, s: jax.random.normal(k, shape, jnp.float32) * s
    D = D_MODEL
    qkv_dim = ATTN_DIM + 2 * ATTN_KV_HEADS * HEAD_DIM
    return {
        'x_prompt': nrm(ks[0], (BATCH, SEQ, D), 1.0),
        'x_sample': nrm(ks[1], (DEC_BATCH, DEC_SEQ, D), 1.0),
        'cache_k': nrm(ks[2], (DEC_BATCH, N_ATTN_LAYERS, PAST_LEN, ATTN_KV_HEADS, HEAD_DIM), 1.0),
        'cache_v': nrm(ks[3], (DEC_BATCH, N_ATTN_LAYERS, PAST_LEN, ATTN_KV_HEADS, HEAD_DIM), 1.0),
        'state_hgrn': nrm(ks[4], (DEC_BATCH, N_HGRN_LAYERS, 2, HGRN_HEADS, HGRN_DK, HGRN_DV), 0.5),
        'c': nrm(ks[5], (DEC_BATCH, D), 1.0),
        'c_ctx': nrm(ks[6], (D,), 1.0),
        'w_ada': nrm(ks[7], (DEPTH, D, N_MOD * D), 0.5 * D ** -0.5),
        'b_ada': nrm(ks[8], (DEPTH, N_MOD * D), 0.01),
        'norm_g': 1.0 + nrm(ks[9], (DEPTH, N_NORMS, D), 0.05),
        'w_ffn_in': nrm(ks[10], (DEPTH, 2, D, 2 * D_FF), D ** -0.5),
        'w_ffn_out': nrm(ks[11], (DEPTH, 2, D_FF, D), D_FF ** -0.5),
        'w_attn_qkv': nrm(ks[12], (N_ATTN_LAYERS, D, qkv_dim), D ** -0.5),
        'w_attn_o': nrm(ks[13], (N_ATTN_LAYERS, ATTN_DIM, D), ATTN_DIM ** -0.5),
        'attn_sink': nrm(ks[14], (N_ATTN_LAYERS, ATTN_HEADS), 1.0),
        'w_conv_in': nrm(ks[15], (N_CONV_LAYERS, D, 3 * D), D ** -0.5),
        'conv_w': nrm(ks[16], (N_CONV_LAYERS, CONV_WIDTH, D), CONV_WIDTH ** -0.5),
        'conv_b': nrm(ks[17], (N_CONV_LAYERS, D), 0.01),
        'w_conv_out': nrm(ks[18], (N_CONV_LAYERS, D, D), D ** -0.5),
        'w_hgrn_in': nrm(ks[19], (N_HGRN_LAYERS, D, 3 * HGRN_FD + 2 * D), D ** -0.5),
        'hgrn_lb': nrm(ks[20], (2, DEPTH, HGRN_FD), 1.0),
        'hgrn_norm_g': 1.0 + nrm(ks[21], (N_HGRN_LAYERS, HGRN_DV), 0.05),
        'w_hgrn_out': nrm(ks[22], (N_HGRN_LAYERS, D, D), D ** -0.5),
    }

def reference(x_prompt, x_sample, cache_k, cache_v, state_hgrn, c, c_ctx, w_ada, b_ada, norm_g,
              w_ffn_in, w_ffn_out, w_attn_qkv, w_attn_o, attn_sink, w_conv_in, conv_w, conv_b,
              w_conv_out, w_hgrn_in, hgrn_lb, hgrn_norm_g, w_hgrn_out):
    yp, ys = x_prompt, x_sample
    Bp = x_prompt.shape[0]
    Bs = x_sample.shape[0]
    new_k, new_v, new_s = [], [], []
    for li in range(DEPTH):
        kind, j = li % N_MIXERS, li // N_MIXERS
        mp = adaln(c_ctx[None, :], w_ada[li], b_ada[li])
        ms = adaln(c, w_ada[li], b_ada[li])
        g = norm_g[li]
        yp = ffn_sublayer(yp, mp[0], mp[1], mp[2], g[0], g[1], w_ffn_in[li, 0], w_ffn_out[li, 0])
        ys = ffn_sublayer(ys, ms[0], ms[1], ms[2], g[0], g[1], w_ffn_in[li, 0], w_ffn_out[li, 0])
        hp = modulate(rmsnorm(yp, g[2]), mp[3], mp[4])
        hs = modulate(rmsnorm(ys, g[2]), ms[3], ms[4])
        if kind == 0:
            op, kc, vc = attn_context(hp, w_attn_qkv[j], w_attn_o[j], attn_sink[j])
            os_ = attn_latent(hs, w_attn_qkv[j], w_attn_o[j], attn_sink[j], cache_k[:, j], cache_v[:, j])
            new_k.append(kc)
            new_v.append(vc)
        elif kind == 1:
            op = short_conv(hp, w_conv_in[j], conv_w[j], conv_b[j], w_conv_out[j])
            os_ = short_conv(hs, w_conv_in[j], conv_w[j], conv_b[j], w_conv_out[j])
        else:
            lb_f = hgrn_lower_bound(hgrn_lb[0], li)
            lb_b = hgrn_lower_bound(hgrn_lb[1], li)
            z0 = jnp.zeros((Bp, HGRN_HEADS, HGRN_DK, HGRN_DV), jnp.float32)
            op, sf, sb = hgrn_mixer(hp, w_hgrn_in[j], lb_f, lb_b, hgrn_norm_g[j], w_hgrn_out[j], z0, z0)
            os_, _, _ = hgrn_mixer(hs, w_hgrn_in[j], lb_f, lb_b, hgrn_norm_g[j], w_hgrn_out[j],
                                   state_hgrn[:, j, 0], state_hgrn[:, j, 1])
            new_s.append(jnp.stack([sf, sb], axis=1))
        yp = yp + mp[5] * rmsnorm(op, g[3])
        ys = ys + ms[5] * rmsnorm(os_, g[3])
        yp = ffn_sublayer(yp, mp[6], mp[7], mp[8], g[4], g[5], w_ffn_in[li, 1], w_ffn_out[li, 1])
        ys = ffn_sublayer(ys, ms[6], ms[7], ms[8], g[4], g[5], w_ffn_in[li, 1], w_ffn_out[li, 1])
    new_cache_k = jnp.stack(new_k, axis=1)
    new_cache_v = jnp.stack(new_v, axis=1)
    new_state_hgrn = jnp.stack(new_s, axis=1)
    return (yp, ys, new_cache_k, new_cache_v, new_state_hgrn)


_drawn_inputs = setup_inputs


def setup_inputs(seed=0):
    import zlib

    import numpy as np

    out = dict(_drawn_inputs(seed))
    spreads = {}
    factors = {'state_hgrn': 8.0, 'attn_sink': 8.0, 'conv_b': 22.205, 'hgrn_norm_g': 17.066}
    for name, (base, spread) in spreads.items():
        noise = np.random.default_rng([zlib.crc32(name.encode()), seed]).standard_normal(out[name].shape)
        drawn = base * np.exp(spread * noise) if base else spread * noise
        out[name] = jnp.asarray(drawn.astype(out[name].dtype))
    for name, factor in factors.items():
        out[name] = (out[name] * factor).astype(out[name].dtype)
    return out
```

```python
from contextlib import ExitStack

import numpy as np

import concourse.bass as bass
from concourse import mybir

F32 = mybir.dt.float32
F32R = mybir.dt.float32r
I32 = mybir.dt.int32
ALU = mybir.AluOpType
ACT = mybir.ActivationFunctionType
AX_X = mybir.AxisListType.X

P = 128
D = 1024
DC = D // P
TP, TS = 128, 256
T = TP + TS
NT = T // P
DEPTH = 4
D_FF = 2816
FC = D_FF // P
N_MOD, N_NORMS = 9, 6
HEADS, KVH, HD = 16, 4, 64
EPS = 1e-6
GROUPS = ((0, TP), (TP, T))
GRID_W = 64
WINDOW = 128
HG = 8
HT = 11
SLOT = HT * P
ADA_COLS = 2 * P
ADA_ALL = DEPTH * N_MOD * D // ADA_COLS
ADA_FIRST = 2 * D // ADA_COLS
LEVELS = 7
CREDIT = 4
OUT_KINDS = ("ffn_out", "mix_out")


def host_constants():
    ident = np.eye(P, dtype=np.float32)
    sel = np.zeros((P, 2), np.float32)
    for g in range(4):
        for c in range(2):
            sel[32 * g + c, c] = 1.0
    m = np.arange(P)
    rot = np.zeros((P, P), np.float32)
    rot[m ^ 32, m] = 1.0
    dup = np.zeros((P, 2, P), np.float32)
    duprot = np.zeros((P, 2, P), np.float32)
    for g in range(2):
        dup[64 * g + m % 64, g, m] = 1.0
        duprot[64 * g + ((m % 64) ^ 32), g, m] = 1.0
    inv = (np.float32(10000.0) ** (-np.arange(16, dtype=np.float32) / np.float32(16))).astype(np.float32)
    tok = np.arange(TS)
    row, col = (tok // GRID_W).astype(np.float32), (tok % GRID_W).astype(np.float32)
    ang = np.concatenate([row[:, None] * inv, col[:, None] * inv], axis=-1)
    cos, sin = np.cos(ang)[:, m % 32].T, np.sin(ang)[:, m % 32].T
    sign = np.where((m % 64) < 32, -1.0, 1.0)[:, None]
    band = np.zeros((P, 2, 3, P), np.float32)
    for n in range(2):
        for kt in range(2):
            off = (n * P + m[:, None]) - (kt * P + m[None, :])
            band[:, n, kt, :] = np.where(np.abs(off) <= WINDOW, 0.0, -1e30)
    attn = np.concatenate([rot, dup.reshape(P, -1), duprot.reshape(P, -1), cos, sin * sign,
                           band[:, 0].reshape(P, -1), np.zeros((P, P)), band[:, 1].reshape(P, -1)],
                          axis=1).astype(np.float32)
    masks = np.zeros((P, 2, 5, 32), np.float32)
    k, q = m[:, None] % 32, np.arange(32)[None, :]
    for lv in range(5):
        kb, qb = k >> lv, q >> lv
        masks[:, 0, lv] = ((kb % 2 == 0) & (qb == kb + 1))
        masks[:, 1, lv] = ((qb % 2 == 0) & (kb == qb + 1))
    base = np.concatenate([ident, sel], axis=1).astype(np.float32)
    return {"k_base": base, "k_attn": np.ascontiguousarray(attn), "k_masks": masks.reshape(P, -1)}


class Phase:

    def __init__(self, s, kind, groups, tiles, src, moving, ada):
        self.s, self.kind, self.groups, self.tiles = s, kind, groups, tiles
        self.src, self.moving, self.ada = src, moving, ada
        self.block0 = 0
        self.use0 = [0] * 4
        self.ada0 = 0


def build(nc, ins, outs, n_sub=12):
    W = ins
    sub_kind = ["ffn", "attn", "ffn", "ffn", "conv", "ffn", "ffn", "hgrn", "ffn", "ffn", "attn", "ffn"][:n_sub]
    N_SUB = len(sub_kind)

    def cols_of(w, first):
        v = w.rearrange("(k p) n -> p k n", p=P)
        return lambda i, j: v[:, :, bass.ds(first(i, j), P)]

    def phases_of(s):
        layer, kind = s // 3, sub_kind[s]
        out = []
        if kind == "ffn":
            f = (s % 3) // 2
            w_in, w_out = W["w_ffn_in"][layer, f], W["w_ffn_out"][layer, f]
            last = s == 11
            out.append(Phase(s, "ffn_in", FC // 2, DC,
                             cols_of(w_in, lambda i, j: i * 2 * P + (j // 2) * P + (j % 2) * D_FF), "h", not last))
            halves = [w_out[h * HT * P:(h + 1) * HT * P, :].rearrange("(k p) n -> p k n", p=P) for h in range(2)]
            out.append(Phase(s, "ffn_out", DC // 2, HT,
                             lambda i, j: halves[j % 2][:, :, bass.ds(i * 2 * P + (j // 2) * P, P)], "h2", not last))
            return out
        if kind == "attn":
            out.append(Phase(s, "qkv", 3, DC, cols_of(W["w_attn_qkv"][s // 9], lambda i, j: i * 4 * P + j * P), "h", True))
            w_out = W["w_attn_o"][s // 9]
        elif kind == "conv":
            w_in = W["w_conv_in"][0]
            out.append(Phase(s, "conv_z", 4, DC,
                             cols_of(w_in, lambda i, j: i * 2 * P + (j // 2) * P + D + (j % 2) * D), "h", True))
            out.append(Phase(s, "conv_g", 2, DC, cols_of(w_in, lambda i, j: i * 4 * P + j * P), "h", True))
            w_out = W["w_conv_out"][0]
        else:
            w_in = W["w_hgrn_in"][0]
            for n, name in enumerate(("hgrn_q", "hgrn_v", "hgrn_ff", "hgrn_fb", "hgrn_g")):
                out.append(Phase(s, name, 2, DC,
                                 cols_of(w_in, lambda i, j, n=n: i * 4 * P + j * P + n * D), "h", n < 3))
            w_out = W["w_hgrn_out"][0]
        out.append(Phase(s, "mix_out", 2, DC, cols_of(w_out, lambda i, j: i * 4 * P + j * P), "o", False))
        return out

    core_ada = {1: 6, 10: 7}
    phases, block, uses, ada = [], 0, [0] * 4, ADA_FIRST
    core_ada0 = {}
    for s in range(N_SUB):
        mine = phases_of(s)
        for ph in mine:
            if ph.kind == "mix_out" and s in core_ada:
                core_ada0[s] = ada
                ada += core_ada[s]
            ph.block0, ph.use0, ph.ada0 = block, list(uses), ada
            block += 4 * ph.groups
            for x in range(4):
                if ph.kind not in OUT_KINDS:
                    uses[x] += ph.groups
            if ph.ada:
                ada += ph.groups
        phases.append(mine)
    flat = [ph for mine in phases for ph in mine]
    following = {id(a): b for a, b in zip(flat, flat[1:] + [None])}
    assert ada <= ADA_ALL and (N_SUB < 12 or ada == ADA_ALL)

    def mods_needed(s, which):
        return (s // 3 * N_MOD + (s % 3) * 3 + which + 1) * DC // 2

    def mod_col(s, which):
        return (s // 3 * N_MOD + (s % 3) * 3 + which) * DC

    def norm_col(s, post):
        return (s // 3 * N_NORMS + (s % 3) * 2 + post) * DC

    at = [16544]
    end_of_sbuf = 229344

    def place(name, shape, dt, offset=None):
        size = int(np.prod(shape[1:])) * 4
        size = (size + 31) // 32 * 32
        if offset is None:
            offset = at[0]
            at[0] += size
            assert at[0] <= end_of_sbuf, (name, at[0])
        return nc.alloc_sbuf_tensor_at(name, shape, dt, offset=offset)

    def pool_of(*spans):
        spans = [list(x) for x in spans]

        def put(name, shape, dt=F32):
            size = (int(np.prod(shape[1:])) * 4 + 31) // 32 * 32
            for sp in spans:
                if sp[0] + size <= sp[1]:
                    sp[0] += size
                    return place(name, shape, dt, sp[0] - size)
            raise ValueError(name)
        return put

    y = place("y", [P, DC, T], F32)
    h_at = at[0]
    h_hi = place("h_hi", [P, DC, T], F32R)
    h_lo = place("h_lo", [P, DC, T], F32R)
    h_end = at[0]
    og = place("og", [P, DC, T], F32, h_at)
    x_at = at[0]
    h2_hi = place("h2_hi", [P, FC, T], F32R)
    h2_mid = at[0]
    h2_lo = place("h2_lo", [P, FC, T], F32R)
    x_end = at[0]
    raw = place("raw", [P, 4, SLOT], F32)
    w_hi = place("w_hi", [P, 4, SLOT], F32R)
    w_lo = place("w_lo", [P, 4, SLOT], F32R)
    ada_raw = place("ada_raw", [P, 2, DC // 2, ADA_COLS], F32)
    ada_rows = place("ada_rows", [P, ADA_COLS], F32)
    tmp = place("tmp", [P, 4, T], F32)
    sq = place("sq", [P, 2, T], F32)
    acc = place("acc", [P, T], F32)
    diag = place("diag", [P, NT, P], F32)
    base_k = place("base_k", [P, P + 2], F32)
    ident, sel = base_k[:, 0:P], base_k[:, P:P + 2]
    ones = place("ones", [P, P], F32)
    mod = place("mod", [P, DEPTH * N_MOD * DC, 2], F32)
    b_cols = place("b_cols", [P, DEPTH * N_MOD * DC], F32)
    g_cols = place("g_cols", [P, DEPTH * N_NORMS * DC], F32)
    misc = place("misc", [P, 113], F32)
    CW, CB, CC, CX, LB, NG = 0, 24, 32, 40, 48, 112
    cond = place("cond", [P, DC, 32], F32)
    s_cols = place("s_cols", [P, DC, 2], F32)
    g_out = place("g_out", [P, DC, 2], F32)
    small = place("small", [P, 16], F32)
    r_var, r_std, m_half, one_k = small[:, 0:3], small[:, 3:6], small[:, 6:9], small[:, 9:10]
    free_at = at[0]

    psum_stack = ExitStack()
    psum = [psum_stack.enter_context(nc.psum_tensor(f"bank{n}", [P, 512], F32)) for n in range(8)]
    ADA_ACC, ADA_T, STAT, SPREAD = 4, 5, 6, 7

    sem_stack = ExitStack()

    def sem(name):
        return sem_stack.enter_context(nc.semaphore(name))

    raw_landed = [sem(f"raw_landed{n}") for n in range(4)]
    w_hi_made, w_lo_made, block_done = sem("w_hi_made"), sem("w_lo_made"), sem("block_done")
    bank_free = [sem(f"bank_free{n}") for n in range(4)]
    ada_landed = [sem(f"ada_landed{n}") for n in range(2)]
    ada_used = [sem(f"ada_used{n}") for n in range(2)]
    ada_copied, ada_turned, mods_made = sem("ada_copied"), sem("ada_turned"), sem("mods_made")
    h2_hi_made, h2_lo_made = sem("h2_hi_made"), sem("h2_lo_made")
    sq_out_made, acc_made = sem("sq_out_made"), sem("acc_made")
    stat_done, var_made, std_made, diag_made, spread_done = (
        sem("stat_done"), sem("var_made"), sem("std_made"), sem("diag_made"), sem("spread_done"))
    t_made, y_made_v, y_made_p, y_sq_made, y_sq_used = (
        sem("t_made"), sem("y_made_v"), sem("y_made_p"), sem("y_sq_made"), sem("y_sq_used"))
    u_made, hm_made, h_hi_made, h_lo_made = sem("u_made"), sem("hm_made"), sem("h_hi_made"), sem("h_lo_made")
    s_ready, g_ready, cols_step = sem("s_ready"), sem("g_ready"), sem("cols_step")
    consts_in, consts_set, started = sem("consts_in"), sem("consts_set"), sem("started")
    vec_in, x_in = sem("vec_in"), sem("x_in")
    turn_done, turn_copied_v, turn_copied_a = sem("turn_done"), sem("turn_copied_v"), sem("turn_copied_a")
    cond_made, acc_zeroed = sem("cond_made"), sem("acc_zeroed")
    out_stored = sem("out_stored")

    def h2_base(s):
        return FC * sub_kind[:s].count("ffn")

    def stores_until(s):
        return 2 * sub_kind[:s].count("attn")

    def loop(eng, n, body):
        if n == 1:
            body(0)
        elif n > 1:
            with eng.Fori(0, n) as i:
                body(i)

    put = pool_of((x_at, x_end))
    xin = put("xin", [P, NT, D])
    vin = put("vin", [P, 6, P])
    VEC_ROWS = (128, 128, 32, 128, 64, 113)
    put = pool_of((x_at, x_end))
    yout = put("yout", [P, NT, D])


    TURNS_START, TURNS_END = 6 + DC, 2 * NT
    TURN_V_END = (TURNS_START + TURNS_END) // 2
    TURN_A_END = (TURNS_START + TURNS_END) // 2

    mix_hi_made, o_lo_made = sem("mix_hi_made"), sem("o_lo_made")
    o_hi, o_lo = h2_hi[:, 0:DC, :], h2_hi[:, DC:2 * DC, :]
    span = (x_at + 2 * 4 * DC * T, x_end)
    moving_of = {"h": (h_hi, h_lo), "h2": (h2_hi, h2_lo), "o": (o_hi, o_lo)}

    def mixer_number(s):
        return s // 3

    SEG = (T, P, T)
    SEG_AT = (0, T, T + P)
    KEYS = sum(SEG)
    KT_ALL = KEYS // P
    SCALE = HD ** -0.5
    put = pool_of(span)
    qkv = put("qkv", [P, 12, T])
    kc = put("kc", [P, KVH, P])
    vc = put("vc", [P, KVH * HD])
    kd = put("kd", [P, KVH, T])
    vt = put("vt", [P, NT, KVH * HD])
    attn_k = put("attn_k", [P, 5 * P + 2 * TS + KEYS])
    kc_raw = put("kc_raw", [P, KVH, 2, HD])
    rope_tmp = put("rope_tmp", [P, 2, TS])
    put = pool_of((h_at, h_end))
    sm = put("sm", [P, 2, KEYS])
    pr = put("pr", [P, 2, KEYS])
    pt = put("pt", [P, 2, KEYS])
    put = pool_of((free_at, end_of_sbuf))
    sink = put("sink", [P, HEADS])
    sink8 = put("sink8", [P, HEADS])
    k_new = put("k_new", [P, KVH * HD])
    soft = put("soft", [P, 2, 16])
    rot_m = attn_k[:, 0:P]
    dup_m = [attn_k[:, P * (1 + g):P * (2 + g)] for g in range(2)]
    duprot_m = [attn_k[:, P * (3 + g):P * (4 + g)] for g in range(2)]
    cos_t = attn_k[:, 5 * P:5 * P + TS]
    sin_t = attn_k[:, 5 * P + TS:5 * P + 2 * TS]
    band_t = attn_k[:, 5 * P + 2 * TS:]
    ROPE = KVH + DC

    attn_in, attn_turned, attn_turn_copied = sem("attn_in"), sem("attn_turned"), sem("attn_turn_copied")
    rope_rot, k_dup_done, k_dup_copied = sem("rope_rot"), sem("k_dup_done"), sem("k_dup_copied")
    rope_cos, rope_sin, rope_add = sem("rope_cos"), sem("rope_sin"), sem("rope_add")
    sink8_made, score_done, score_read, neg_made = sem("sink8_made"), sem("score_done"), sem("score_read"), sem("neg_made")
    prob_made, soft_step, p_normed, pt_done = sem("prob_made"), sem("soft_step"), sem("p_normed"), sem("pt_done")
    pt_copied_v, pt_copied_a, pv_done = sem("pt_copied_v"), sem("pt_copied_a"), sem("pv_done")
    STEPS = HEADS + 3

    def attn_number(s):
        return s // 9

    def ada_at_step(s, st):
        n = (st - 2) // 2
        return core_ada0[s] + n if st >= 2 and st % 2 == 0 and n < core_ada[s] else None

    put = pool_of(span)
    conv_z = put("conv_z", [P, DC, T])
    conv_r = put("conv_r", [P, DC, T])
    conv_step = sem("conv_step")

    HKIND = {"hgrn_q": 0, "hgrn_ff": 1, "hgrn_fb": 2, "hgrn_g": 3}
    LOW = 5
    PAIRS = HG // 2
    DIRS = 2
    hg_f = [place("hg_ff", [P, HG, T], F32, x_at),
            place("hg_fb", [P, HG, T], F32, x_at + 4 * DC * T)]
    put = pool_of(span)
    hg_q = put("hg_q", [P, HG, T])
    hg_v = put("hg_v", [P, HG, T])
    hg_g = put("hg_g", [P, HG, T])
    hg_kr = [put(f"hg_kr{z}", [P, DIRS, T]) for z in range(2)]
    put = pool_of((h_at, h_end), (free_at, end_of_sbuf))
    hg_qp = [put(f"hg_qp{z}", [P, DIRS, T]) for z in range(2)]
    DECAYS = [2 * T - (2 * T >> lv) - T for lv in range(1, LEVELS + 2)]
    hg_t = [put(f"hg_t{z}", [P, DIRS, DECAYS[-1]]) for z in range(2)]
    hg_ks = [put(f"hg_ks{z}", [P, T]) for z in range(2)]
    hg_vt = [put(f"hg_vt{z}", [P, NT, P]) for z in range(2)]
    hg_s = [put(f"hg_s{z}", [P, T]) for z in range(2)]
    hg_x = [put(f"hg_x{z}", [P, DIRS, P]) for z in range(2)]
    hg_vh = [put(f"hg_vh{z}", [P, T]) for z in range(2)]
    hg_kt = [put(f"hg_kt{z}", [P, DIRS, P]) for z in range(2)]
    hg_in = [put(f"hg_in{z}", [P, DIRS, P]) for z in range(2)]
    hg_out = [put(f"hg_out{z}", [P, DIRS, P]) for z in range(2)]
    hg_o2, hg_r = hg_ks, hg_vh
    hg_qh = hg_s
    hg_low = [put(f"hg_low{z}", [P, NT, 32]) for z in range(2)]
    hg_mask = put("hg_mask", [P, DIRS, LOW, 32])
    hg_lb = put("hg_lb", [P, 8, DIRS * HG])
    lb_exp = put("lb_exp", [P, DIRS, DEPTH, HG])
    SCORE, HIGH, BYTOKEN, OUT = 0, 2, 4, 6

    def per_slot(name):
        return [sem(f"{name}{z}") for z in range(2)]

    mask_in, lb_step, sig_made = sem("mask_in"), sem("lb_step"), sem("sig_made")
    k_init, vh_made, v_turned, vt_copied = per_slot("k_init"), per_slot("vh_made"), per_slot("v_turned"), per_slot("vt_copied")
    Q_AT = [2 + 2 * lv + 2 * min(lv, LOW) for lv in range(LEVELS + 1)]
    Q_STEPS, K_STEPS, T_STEPS, SCORE_STEPS = Q_AT[LEVELS] + 2, 1 + 2 * LEVELS, LEVELS + 1, LEVELS + 1
    q_step, k_step, t_step, scr_done = per_slot("q_step"), per_slot("k_step"), per_slot("t_step"), per_slot("scr_done")
    diag_copied, s_copied, x_copied = per_slot("diag_copied"), per_slot("s_copied"), per_slot("x_copied")
    kr_turned, kt_copied, st_done, st_copied = (
        per_slot("kr_turned"), per_slot("kt_copied"), per_slot("st_done"), per_slot("st_copied"))
    o_done, o2_made, o_var, var_read, root_made, o_step = (
        per_slot("o_done"), per_slot("o2_made"), per_slot("o_var"), per_slot("var_read"), per_slot("root_made"),
        per_slot("o_step"))
    state_in, state_stored = per_slot("state_in"), per_slot("state_stored")

    def sp_core_start(sp, s):
        if sub_kind[s] == "attn":
            a = attn_number(s)
            sp.wait_ge(block_done, phases[s][0].block0 + CREDIT)
            sp.dma_start(attn_k[:, :], ins["k_attn"]).then_inc(attn_in, 16)
            ck = W["cache_k"][0, a].rearrange("s g d -> s g d")
            sp.dma_start(kc_raw[:, :, 0, :], ck).then_inc(attn_in, 16)
            sp.dma_start(kc_raw[:, :, 1, :], ck).then_inc(attn_in, 16)
            sp.dma_start(vc[:, :], W["cache_v"][0, a].rearrange("s g d -> s (g d)")).then_inc(attn_in, 16)
            sp.dma_start(sink[:, :], W["attn_sink"][a:a + 1, :].to_broadcast([P, HEADS])).then_inc(attn_in, 16)
        elif sub_kind[s] == "hgrn":
            sp_hgrn_start(sp, s)

    def sp_core(sp, s, load_ada, ada_layer):
        if sub_kind[s] == "attn":
            a = attn_number(s)
            sp.wait_ge(attn_turn_copied, 5 * a + 4)
            sp.dma_start(outs["new_k"][0, a].rearrange("s g d -> s (g d)"), k_new[:, :]).then_inc(out_stored, 16)
            sp.dma_start(outs["new_v"][0, a].rearrange("s g d -> s (g d)"), vt[:, 0, :]).then_inc(out_stored, 16)
            for n in range(core_ada0[s], core_ada0[s] + core_ada[s]):
                ada_layer[0] = n // (N_MOD * D // ADA_COLS)
                load_ada(n)
        elif sub_kind[s] == "hgrn":
            sp_hgrn_core(sp, s)

    def pe_core(pe, s, ada_products, ada_turn):
        mm = nc.tensor.matmul
        out_phase = phases[s][-1]
        for x in range(4):
            pe.wait_ge(bank_free[x], out_phase.use0[x] + 1)
        if sub_kind[s] == "hgrn":
            pe_hgrn_core(pe, s)
        if sub_kind[s] != "attn":
            return
        a = attn_number(s)
        mi = mixer_number(s)
        pe.wait_ge(attn_in, 16 * 5 * (a + 1))

        def turn(bank, sources):
            for q, src in enumerate(sources):
                last = nc.tensor.transpose(psum[bank][:, q * P:(q + 1) * P], src, ident)
            last.then_inc(attn_turned, 1)

        for t in range(NT):
            turn(t, [qkv[:, 10 + c, t * P:(t + 1) * P] for c in range(2)])
        turn(3, [qkv[:, 8 + c, 0:P] for c in range(2)])
        pe.wait_ge(attn_turn_copied, 5 * a + 1)
        turn(0, [kc_raw[:, g, :, :].rearrange("p a d -> p (a d)") for g in range(KVH)])
        pe.wait_ge(attn_turn_copied, 5 * a + 5)
        for r in range(ROPE):
            done = ROPE * a + r
            if r < KVH:
                if r >= 2:
                    pe.wait_ge(k_dup_copied, KVH * a + r - 1)
                mm(psum[r % 2][:, 0:T], dup_m[r % 2], qkv[:, 8 + r // 2, :], start=True,
                   stop=True).then_inc(k_dup_done, 1)
            if r >= 2:
                pe.wait_ge(rope_sin, done - 1)
            stat, src = (duprot_m[r % 2], qkv[:, 8 + r // 2, TP:T]) if r < KVH else (rot_m, qkv[:, r - KVH, TP:T])
            mm(psum[2 + r % 2][:, 0:TS], stat, src, start=True, stop=True).then_inc(rope_rot, 1)

        def scores(h):
            n = HEADS * a + h
            lo, g = HD * (h % 2), h // (HEADS // KVH)
            half = slice(lo, lo + HD)
            pe.wait_ge(rope_add, ROPE * a + KVH + h // 2 + 1)
            if h == 0:
                pe.wait_ge(k_dup_copied, KVH * (a + 1))
            else:
                pe.wait_ge(score_read, n)
            q = [qkv[half, h // 2, t * P:(t + 1) * P] for t in range(NT)]
            mm(psum[0][:, 0:TS], q[1], kd[half, g, TP:T], start=True, stop=True)
            mm(psum[0][:, TS:T], q[1], kc[half, g, :], start=True, stop=True)
            mm(psum[0][:, T:T + P], q[0], kd[half, g, 0:TP], start=True, stop=True)
            mm(psum[1][:, 0:TS], q[2], kd[half, g, TP:T], start=True, stop=True)
            mm(psum[1][:, TS:T], q[2], kc[half, g, :], start=True, stop=True).then_inc(score_done, 1)

        def turn_probs(h):
            n = HEADS * a + h
            pe.wait_ge(p_normed, n + 1)
            if h == 0:
                pe.wait_ge(rope_sin, ROPE * (a + 1))
            else:
                pe.wait_ge(pt_copied_v, n)
                pe.wait_ge(pt_copied_a, n)
            for k in range(KT_ALL):
                last = nc.tensor.transpose(psum[2 + k // 4][:, k % 4 * P:(k % 4 + 1) * P],
                                           pr[:, h % 2, k * P:(k + 1) * P], ident)
            last.then_inc(pt_done, 1)

        def values(h):
            n = HEADS * a + h
            c, lo, g = h // 2, HD * (h % 2), h // (HEADS // KVH)
            pe.wait_ge(pt_copied_v, n + 1)
            pe.wait_ge(pt_copied_a, n + 1)
            if h % 2 == 0 and c >= 2:
                pe.wait_ge(o_lo_made, DC * mi + c - 1 + CREDIT)
            bank = psum[6 + c % 2][lo:lo + HD, :]
            cols = slice(g * HD, (g + 1) * HD)
            key = [vt[:, 1, cols], vt[:, 2, cols], vc[:, cols]]
            mm(bank[:, 0:P], vt[:, 0, cols], pt[:, h % 2, 3 * P:4 * P], start=True, stop=True, tile_position=(0, lo))
            for blk in range(2):
                for k in range(3):
                    kt = 4 * blk + k
                    last = mm(bank[:, (1 + blk) * P:(2 + blk) * P], key[k], pt[:, h % 2, kt * P:(kt + 1) * P],
                              start=(k == 0), stop=(k == 2), tile_position=(0, lo))
            last.then_inc(pv_done, 1)

        for st in range(STEPS):
            ada = ada_at_step(s, st)
            if ada is not None:
                ada_products(ada)
            if st < HEADS:
                scores(st)
            if 1 <= st <= HEADS:
                turn_probs(st - 1)
            if ada is not None:
                ada_turn(ada)
            if 2 <= st <= HEADS + 1:
                values(st - 2)

    def act_mix(act, ph, i, half):
        A = nc.scalar.activation
        ja, jb = 2 * half, 2 * half + 1
        block = ph.block0 + 4 * i
        if ph.kind == "qkv":
            for j in (ja, jb):
                act.wait_ge(block_done, block + j + 1 + CREDIT)
                A(qkv[:, 4 * i + j, :], psum[j][:, 0:T], ACT.Copy).then_inc(bank_free[j], 1)
        elif ph.kind == "conv_z":
            act.wait_ge(block_done, block + ja + 1 + CREDIT)
            act.wait_ge(bank_free[jb], ph.use0[jb] + i + 1)
            A(tmp[:, half, :], psum[ja][:, 0:T], ACT.Copy).then_inc(bank_free[ja], 1)
        elif ph.kind.startswith("hgrn"):
            act_hgrn_mix(act, ph, i, half)

    def act_core(act, s, ada_copy):
        A = nc.scalar.activation
        if sub_kind[s] == "hgrn":
            act_hgrn_core(act, s)
        if sub_kind[s] != "attn":
            return
        a = attn_number(s)
        mi = mixer_number(s)
        for n in range(5):
            act.wait_ge(attn_turned, 5 * a + n + 1)
            dst = (vt[:, n, :] if n < NT else k_new[:, :] if n == NT else kc[:, :, :].rearrange("p g s -> p (g s)"))
            A(dst, psum[n % 4][:, 0:(512 if n == 4 else 256)], ACT.Copy).then_inc(attn_turn_copied, 1)
        for g in range(KVH):
            act.wait_ge(k_dup_done, KVH * a + g + 1)
            A(kd[:, g, :], psum[g % 2][:, 0:T], ACT.Copy).then_inc(k_dup_copied, 1)
        for st in range(STEPS + 1):
            ada = ada_at_step(s, st)
            if ada is not None:
                ada_copy(ada)
            if 1 <= st <= HEADS:
                h = st - 1
                act.wait_ge(pt_done, HEADS * a + h + 1)
                if h >= 2:
                    act.wait_ge(pv_done, HEADS * a + h - 1)
                A(pt[:, h % 2, 512:KEYS], psum[3][:, 0:KEYS - 512], ACT.Copy).then_inc(pt_copied_a, 1)
            if st < HEADS:
                h = st
                act.wait_ge(neg_made, HEADS * a + h + 1)
                if h >= 2:
                    act.wait_ge(pt_done, HEADS * a + h - 1)
                neg = soft[:, h % 2, 3:6]
                for g in range(3):
                    seg = slice(SEG_AT[g], SEG_AT[g] + SEG[g])
                    A(pr[:, h % 2, seg], sm[:, h % 2, seg], ACT.Exp, bias=neg[:, g:g + 1], scale=SCALE,
                      accum_out=soft[:, h % 2, 6 + g:7 + g])
                A(soft[:, h % 2, 9:12], neg, ACT.Exp, bias=sink[:, h:h + 1]).then_inc(prob_made, 1)
            if st >= 4 and st % 2 == 0:
                c = st // 2 - 2
                act.wait_ge(pv_done, HEADS * a + 2 * c + 2)
                A(o_hi[:, c, :], psum[6 + c % 2][:, 0:T], ACT.Copy).then_inc(mix_hi_made, 1)

    def dve_mix(dve, ph, i, half):
        V = nc.vector
        ja, jb = 2 * half, 2 * half + 1
        block = ph.block0 + 4 * i
        if ph.kind == "conv_z":
            c = 2 * i + half
            dve.wait_ge(bank_free[ja], ph.use0[ja] + i + 2)
            dve.wait_ge(block_done, block + jb + 1 + CREDIT)
            V.tensor_tensor(conv_z[:, c, :], psum[jb][:, 0:T], tmp[:, half, :], ALU.mult).then_inc(bank_free[jb], 1)
            dve.wait_ge(bank_free[jb], ph.use0[jb] + i + 2)
            z, r = conv_z[:, c, :], conv_r[:, c, :]

            def tap(j):
                return misc[:, bass.ds(CW + j * DC + c, 1)]
            V.tensor_scalar(r, z, tap(1), misc[:, bass.ds(CB + c, 1)], ALU.mult, ALU.add).then_inc(conv_step, 1)
            n = 5 * c + 1
            for q, (j, (lo, hi)) in enumerate([(0, g) for g in GROUPS] + [(2, g) for g in GROUPS]):
                dve.wait_ge(conv_step, n + (0 if q == 0 else q - 1))
                dst, src = (slice(lo + 1, hi), slice(lo, hi - 1)) if j == 0 else (slice(lo, hi - 1), slice(lo + 1, hi))
                V.scalar_tensor_tensor(out=conv_r[:, c, dst], in0=conv_z[:, c, src], scalar=tap(j),
                                       in1=conv_r[:, c, dst], op0=ALU.mult, op1=ALU.add).then_inc(conv_step, 1)
        elif ph.kind == "conv_g":
            for j in (ja, jb):
                c = 4 * i + j
                dve.wait_ge(block_done, block + j + 1 + CREDIT)
                dve.wait_ge(o_lo_made, DC * mixer_number(ph.s) + c + 1)
                if j < 2:
                    dve.wait_ge(conv_step, 5 * DC)
                V.tensor_tensor(tmp[:, j, :], psum[j][:, 0:T], conv_r[:, c, :], ALU.mult).then_inc(bank_free[j], 1)
                dve.wait_ge(bank_free[j], ph.use0[j] + i + 2)
                V.tensor_copy(o_hi[:, c, :], tmp[:, j, :]).then_inc(mix_hi_made, 1)
        elif ph.kind.startswith("hgrn"):
            dve_hgrn_mix(dve, ph, i, half)

    def dve_core(dve, s, mod_add):
        V = nc.vector
        if sub_kind[s] == "hgrn":
            dve_hgrn_core(dve, s)
        if sub_kind[s] != "attn":
            return
        a = attn_number(s)
        mi = mixer_number(s)
        for r in range(ROPE):
            n = ROPE * a + r
            dst = kd[:, r, TP:T] if r < KVH else qkv[:, r - KVH, TP:T]
            dve.wait_ge(rope_rot, n + 1)
            V.tensor_tensor(rope_tmp[:, r % 2, :], psum[2 + r % 2][:, 0:TS], sin_t, ALU.mult).then_inc(rope_sin, 1)
            dve.wait_ge(rope_cos, n + 1)
            dve.wait_ge(rope_sin, n + 1)
            V.tensor_tensor(dst, dst, rope_tmp[:, r % 2, :], ALU.add).then_inc(rope_add, 1)
        dve.wait_ge(sink8_made, a + 1)
        for st in range(STEPS + 1):
            if st < HEADS:
                h = st
                n = HEADS * a + h
                dve.wait_ge(score_done, n + 1)
                if h >= 2:
                    dve.wait_ge(prob_made, n - 1)
                for g in range(3):
                    seg = slice(SEG_AT[g], SEG_AT[g] + SEG[g])
                    src = psum[0][:, seg] if g < 2 else psum[1][:, 0:T]
                    last = V.tensor_tensor_reduce(sm[:, h % 2, seg], src, band_t[:, seg], 1.0, sink8[:, h:h + 1],
                                                  ALU.add, ALU.max, soft[:, h % 2, g:g + 1])
                last.then_inc(score_read, 1)
                dve.wait_ge(score_read, n + 1)
                V.tensor_scalar(soft[:, h % 2, 3:6], soft[:, h % 2, 0:3], -SCALE, None, ALU.mult).then_inc(neg_made, 1)
            ada = ada_at_step(s, st)
            if 1 <= st <= HEADS:
                h = st - 1
                dve.wait_ge(pt_done, HEADS * a + h + 1)
                if h >= 2:
                    dve.wait_ge(pv_done, HEADS * a + h - 1)
                V.tensor_copy(pt[:, h % 2, 0:512], psum[2][:, :]).then_inc(pt_copied_v, 1)
            if st < HEADS:
                h = st
                n = HEADS * a + h
                dve.wait_ge(prob_made, n + 1)
                V.tensor_tensor(soft[:, h % 2, 12:15], soft[:, h % 2, 6:9], soft[:, h % 2, 9:12],
                                ALU.add).then_inc(soft_step, 1)
                dve.wait_ge(soft_step, 2 * n + 1)
                V.reciprocal(soft[:, h % 2, 12:15], soft[:, h % 2, 12:15]).then_inc(soft_step, 1)
                dve.wait_ge(soft_step, 2 * n + 2)
                for g in range(3):
                    seg = slice(SEG_AT[g], SEG_AT[g] + SEG[g])
                    last = V.tensor_scalar(pr[:, h % 2, seg], pr[:, h % 2, seg], soft[:, h % 2, 12 + g:13 + g],
                                           None, ALU.mult)
                last.then_inc(p_normed, 1)
            if ada is not None:
                mod_add(ada)
            if st >= 4 and st % 2 == 0:
                c = st // 2 - 2
                dve.wait_ge(mix_hi_made, DC * mi + c + 1)
                V.tensor_tensor(o_lo[:, c, :], psum[6 + c % 2][:, 0:T], o_hi[:, c, :].bitcast(F32),
                                ALU.subtract).then_inc(o_lo_made, 1)
        dve.wait_ge(out_stored, 16 * stores_until(s + 1))

    def gp_mix(gp, ph, i):
        G = nc.gpsimd
        if ph.kind == "conv_g":
            for j in range(4):
                c = 4 * i + j
                gp.wait_ge(mix_hi_made, DC * mixer_number(ph.s) + c + 1)
                G.tensor_tensor(o_lo[:, c, :], tmp[:, j, :], o_hi[:, c, :].bitcast(F32),
                                ALU.subtract).then_inc(o_lo_made, 1)

    def gp_core(gp, s):
        G = nc.gpsimd
        if sub_kind[s] == "hgrn":
            gp_hgrn_core(gp, s)
        if sub_kind[s] != "attn":
            return
        a = attn_number(s)
        gp.wait_ge(attn_in, 16 * 5 * (a + 1))
        G.tensor_scalar(sink8[:, :], sink[:, :], 1.0 / SCALE, None, ALU.mult).then_inc(sink8_made, 1)
        for r in range(ROPE):
            gp.wait_ge(rope_rot, ROPE * a + r + 1)
            if r < KVH:
                gp.wait_ge(k_dup_copied, KVH * a + r + 1)
            dst = kd[:, r, TP:T] if r < KVH else qkv[:, r - KVH, TP:T]
            G.tensor_tensor(dst, dst, cos_t, ALU.mult).then_inc(rope_cos, 1)

    def halves(ap, b):
        return ap.rearrange("p (n two b) -> p n two b", two=2, b=b)

    def decay(z, d, h, lv, half):
        b = 1 << lv
        v = hg_f[d][:, h, :] if lv == 0 else hg_t[z][:, d, DECAYS[lv - 1]:DECAYS[lv]]
        return v.rearrange("p (n two) -> p n two", two=2)[:, :, half].unsqueeze(2).to_broadcast([P, T // (2 * b), b])

    def sp_hgrn_start(sp, s):
        sp.wait_ge(block_done, phases[s][0].block0 + CREDIT)
        sp.dma_start(hg_mask[:, :, :, :].rearrange("p d l q -> p (d l q)"), ins["k_masks"]).then_inc(mask_in, 16)

    def sp_hgrn_core(sp, s):
        sp.wait_ge(sig_made, 4 * HG)
        for z in range(2):
            sp.sem_inc(state_stored[z], 16)

        def body(i):
            for z in range(2):
                sp.wait_ge(o_done[z], i + 1)
                sp.dma_start(hg_in[z][:, :, :], W["state_hgrn"][0, 0, :, 2 * i + z].rearrange("e d v -> d e v")
                             ).then_inc(state_in[z], 16)
            for z in range(2):
                sp.wait_ge(st_copied[z], i + 2)
                sp.dma_start(outs["new_state"][0, 0, :, 2 * i + z].rearrange("e d v -> d e v"),
                             hg_out[z][:, :, :]).then_inc(state_stored[z], 16)
        loop(sp, PAIRS, body)

    def pe_hgrn_core(pe, s):
        mm = nc.tensor.matmul
        ada = phases[s][-1].ada0
        pe.wait_ge(ada_copied, ada)
        pe.wait_ge(mods_made, ada)
        for z in range(2):
            pe.sem_inc(o_done[z], 1)
            pe.sem_inc(kr_turned[z], 1)
            pe.sem_inc(v_turned[z], 1)

        def blocks32(z, keys, queries, col):
            for t in range(NT):
                for g in range(4):
                    rows = slice(t * P + 32 * g, t * P + 32 * g + 32)
                    last = mm(psum[SCORE + z][32 * g:32 * g + 32, col + 32 * t:col + 32 * t + 32],
                              keys[:, rows], queries[:, rows], start=True, stop=True, tile_position=(0, 32 * g))
            return last

        def level(z, i, lv):
            if lv == 0:
                pe.wait_ge(k_init[z], 2 * i + 2)
            else:
                pe.wait_ge(k_step[z], K_STEPS * i + 1 + 2 * lv)
            pe.wait_ge(q_step[z], Q_STEPS * i + Q_AT[lv] + 1)
            if lv < LOW:
                if lv == 0:
                    pe.wait_ge(diag_copied[z], i + 1)
                for d in range(DIRS):
                    last = blocks32(z, hg_kr[z][:, d, :], hg_qp[z][:, d, :], d * NT * 32)
                last.then_inc(scr_done[z], 1)
                return
            if lv == LOW:
                pe.wait_ge(var_read[z], i + 1)
            b = 1 << lv
            for t in range(NT):
                for n in range(P // b):
                    d = n % 2
                    m = n + 1 - 2 * d
                    last = mm(psum[HIGH + z][n * b:(n + 1) * b, t * P + m * b:t * P + (m + 1) * b],
                              hg_kr[z][:, d, t * P + n * b:t * P + (n + 1) * b],
                              hg_qp[z][:, d, t * P + m * b:t * P + (m + 1) * b],
                              start=True, stop=True, tile_position=(0, n * b))
            last.then_inc(scr_done[z], 1)

        def body(i):
            for z in range(2):
                pe.wait_ge(vh_made[z], 2 * i + 1)
                pe.wait_ge(st_copied[z], i + 1)
                for t in range(NT):
                    last = nc.tensor.transpose(psum[BYTOKEN + z][:, t * P:(t + 1) * P],
                                               hg_vh[z][:, t * P:(t + 1) * P], ident)
                last.then_inc(v_turned[z], 1)
            for z in range(2):
                pe.wait_ge(k_step[z], K_STEPS * i + 1)
                pe.wait_ge(vh_made[z], 2 * i + 2)
                pe.wait_ge(x_copied[z], i + 1)
                blocks32(z, hg_ks[z][:, :], hg_qh[z][:, :], 0).then_inc(scr_done[z], 1)
            for lv in range(LEVELS):
                for z in range(2):
                    level(z, i, lv)
            for z in range(2):
                pe.wait_ge(k_step[z], K_STEPS * (i + 1))
                pe.wait_ge(q_step[z], Q_STEPS * i + Q_AT[LEVELS] + 1)
                for d in range(DIRS):
                    mm(psum[SCORE + z][:, d * P:(d + 1) * P], hg_kr[z][:, d, (1 + d) * P:(2 + d) * P],
                       hg_qp[z][:, d, (2 - d) * P:(3 - d) * P], start=True, stop=True)
                pe.wait_ge(vt_copied[z], i + 1)
                for d in range(DIRS):
                    last = nc.tensor.transpose(psum[BYTOKEN + z][:, d * P:(d + 1) * P], hg_kr[z][:, d, 0:P], ident)
                last.then_inc(kr_turned[z], 1)
            for z in range(2):
                pe.wait_ge(kt_copied[z], i + 1)
                for d in range(DIRS):
                    last = mm(psum[BYTOKEN + z][:, d * P:(d + 1) * P], hg_kt[z][:, d, :], hg_vt[z][:, 0, :],
                              start=True, stop=True)
                last.then_inc(st_done[z], 1)
            for z in range(2):
                pe.wait_ge(state_in[z], 16 * (i + 1))
                pe.wait_ge(q_step[z], Q_STEPS * (i + 1) + 1)
                pe.wait_ge(s_copied[z], 5 * (i + 1))
                pe.wait_ge(x_copied[z], i + 2)
                pe.wait_ge(o_step[z], 2 * i + 1)
                out = psum[OUT + z]
                mm(out[:, 0:P], hg_vt[z][:, 0, :], hg_s[z][:, 0:P], start=True, stop=True)
                for d in range(DIRS):
                    mm(out[:, P:T], hg_in[z][:, d, :], hg_qp[z][:, d, P:T], start=(d == 0), stop=False,
                       skip_group_check=True)
                for t in range(1, NT):
                    mm(out[:, t * P:(t + 1) * P], hg_vt[z][:, t, :], hg_s[z][:, t * P:(t + 1) * P],
                       start=False, stop=False, skip_group_check=True)
                    d = 2 - t
                    last = mm(out[:, t * P:(t + 1) * P], hg_vt[z][:, NT - t, :], hg_x[z][:, d, :],
                              start=False, stop=True, skip_group_check=True)
                last.then_inc(o_done[z], 1)
            for z in range(2):
                pe.wait_ge(o2_made[z], i + 1)
                mm(psum[HIGH + z][:, 0:T], ones[:, :], hg_o2[z][:, :], start=True, stop=True).then_inc(o_var[z], 1)
        loop(pe, PAIRS, body)

    def act_lower_bound(act):
        A = nc.scalar.activation
        act.wait_ge(lb_step, 2)
        A(lb_exp[:, :, :, :], lb_exp[:, :, :, :], ACT.Exp).then_inc(lb_step, 1)

    def act_hgrn_mix(act, ph, i, half):
        A = nc.scalar.activation
        for j in (2 * half, 2 * half + 1):
            act.wait_ge(block_done, ph.block0 + 4 * i + j + 1 + CREDIT)
            if ph.kind == "hgrn_v":
                A(hg_v[:, 4 * i + j, :], psum[j][:, 0:T], ACT.Copy).then_inc(bank_free[j], 1)
            else:
                act.wait_ge(bank_free[j], ph.use0[j] + i + 1)
                A(tmp[:, j, :], psum[j][:, 0:T], ACT.Sigmoid).then_inc(sig_made, 1)

    def act_hgrn_core(act, s):
        A = nc.scalar.activation
        mi = mixer_number(s)
        for z in range(2):
            act.sem_inc(st_copied[z], 1)
            act.sem_inc(x_copied[z], 1)
        for j in range(4):
            act.wait_ge(bank_free[j], phases[s][-1].use0[j] + 1)

        def body(i):
            for z in range(2):
                act.wait_ge(kr_turned[z], i + 1)
                h = 2 * i + z
                for d in range(DIRS):
                    A(hg_kr[z][:, d, :], hg_f[d][:, h, :], ACT.Identity, bias=ones[:, 0:1],
                      scale=-1.0).then_inc(k_init[z], 1)
                act.wait_ge(v_turned[z], i + 1)
                act.wait_ge(o_step[z], 2 * i + 1)
                A(hg_vh[z][:, :], hg_v[:, 2 * i + z, :], ACT.Copy).then_inc(vh_made[z], 1)
                act.wait_ge(o_done[z], i + 1)
                A(hg_qh[z][:, :], hg_q[:, 2 * i + z, :], ACT.Copy).then_inc(vh_made[z], 1)
            for z in range(2):
                act.wait_ge(v_turned[z], i + 2)
                A(hg_vt[z][:, :, :].rearrange("p t v -> p (t v)"), psum[BYTOKEN + z][:, 0:T],
                  ACT.Copy).then_inc(vt_copied[z], 1)
            for z in range(2):
                act.wait_ge(scr_done[z], SCORE_STEPS * i + 1)
                A(hg_low[z][:, :, :].rearrange("p t q -> p (t q)"), psum[SCORE + z][:, 0:NT * 32],
                  ACT.Copy).then_inc(diag_copied[z], 1)
            for z in range(2):
                act.wait_ge(scr_done[z], SCORE_STEPS * i + 1 + LEVELS)
                A(hg_s[z][:, :], psum[HIGH + z][:, 0:T], ACT.Copy).then_inc(s_copied[z], 1)
                act.wait_ge(q_step[z], Q_STEPS * i + Q_AT[LOW] + 1)
                act.wait_ge(s_copied[z], 5 * i + 1)
                for g in range(4):
                    rows = slice(32 * g, 32 * g + 32)
                    A(hg_s[z][rows, :].rearrange("p (t q) -> p t q", t=NT)[:, :, rows], hg_low[z][rows, :, :],
                      ACT.Copy).then_inc(s_copied[z], 1)
            for z in range(2):
                act.wait_ge(kr_turned[z], i + 2)
                A(hg_kt[z][:, :, :].rearrange("p d k -> p (d k)"), psum[BYTOKEN + z][:, 0:2 * P],
                  ACT.Copy).then_inc(kt_copied[z], 1)
                A(hg_x[z][:, :, :].rearrange("p d k -> p (d k)"), psum[SCORE + z][:, 0:2 * P],
                  ACT.Copy).then_inc(x_copied[z], 1)
            for z in range(2):
                act.wait_ge(st_done[z], i + 1)
                act.wait_ge(state_stored[z], 16 * (i + 1))
                A(hg_out[z][:, :, :].rearrange("p d v -> p (d v)"), psum[BYTOKEN + z][:, 0:2 * P],
                  ACT.Copy).then_inc(st_copied[z], 1)
            for z in range(2):
                act.wait_ge(o_done[z], i + 2)
                A(hg_o2[z][:, :], psum[OUT + z][:, 0:T], ACT.Square).then_inc(o2_made[z], 1)
        loop(act, PAIRS, body)

    def dve_lower_bound(dve):
        V = nc.vector
        row = misc[:, LB:LB + DIRS * DEPTH * HG].rearrange("p (d l c) -> p d l c", d=DIRS, l=DEPTH)

        def cols(n):
            return hg_lb[:, n, :].rearrange("p (d c) -> p d c", d=DIRS)
        MAX, SUM, TOP, LOWER, REST = range(5)
        V.tensor_reduce(cols(MAX), row.rearrange("p d l c -> p d c l"), AX_X, ALU.max).then_inc(lb_step, 1)
        dve.wait_ge(lb_step, 1)
        V.tensor_tensor(lb_exp[:, :, :, :], row, cols(MAX).unsqueeze(2).to_broadcast([P, DIRS, DEPTH, HG]),
                        ALU.subtract).then_inc(lb_step, 1)
        dve.wait_ge(lb_step, 3)
        V.tensor_reduce(cols(SUM), lb_exp[:, :, :, :].rearrange("p d l c -> p d c l"), AX_X,
                        ALU.add).then_inc(lb_step, 1)
        V.tensor_tensor(cols(TOP), lb_exp[:, :, 1, :], lb_exp[:, :, 2, :], ALU.add).then_inc(lb_step, 1)
        dve.wait_ge(lb_step, 5)
        V.reciprocal(hg_lb[:, SUM, :], hg_lb[:, SUM, :]).then_inc(lb_step, 1)
        dve.wait_ge(lb_step, 6)
        V.tensor_tensor(hg_lb[:, LOWER, :], hg_lb[:, TOP, :], hg_lb[:, SUM, :], ALU.mult).then_inc(lb_step, 1)
        dve.wait_ge(lb_step, 7)
        V.tensor_scalar(hg_lb[:, REST, :], hg_lb[:, LOWER, :], -1.0, 1.0, ALU.mult, ALU.add).then_inc(lb_step, 1)

    def dve_hgrn_mix(dve, ph, i, half):
        V = nc.vector
        if ph.kind == "hgrn_v":
            return
        for j in (2 * half, 2 * half + 1):
            c = 4 * i + j
            dve.wait_ge(sig_made, HKIND[ph.kind] * HG + c + 1)
            if ph.kind in ("hgrn_ff", "hgrn_fb"):
                d = HKIND[ph.kind] - 1
                dve.wait_ge(lb_step, 8)
                V.tensor_scalar(hg_f[d][:, c, :], tmp[:, j, :], hg_lb[:, 4, bass.ds(d * HG + c, 1)],
                                hg_lb[:, 3, bass.ds(d * HG + c, 1)], ALU.mult, ALU.add).then_inc(bank_free[j], 1)
            elif ph.kind == "hgrn_q":
                V.scalar_tensor_tensor(out=hg_q[:, c, :], in0=psum[j][:, 0:T], scalar=P ** -0.5, in1=tmp[:, j, :],
                                       op0=ALU.mult, op1=ALU.mult).then_inc(bank_free[j], 1)
            else:
                V.tensor_tensor(hg_g[:, c, :], psum[j][:, 0:T], tmp[:, j, :], ALU.mult).then_inc(bank_free[j], 1)

    def dve_hgrn_core(dve, s):
        V = nc.vector
        mi = mixer_number(s)
        for z in range(2):
            dve.sem_inc(q_step[z], 1)
            dve.sem_inc(var_read[z], 1)
            dve.sem_inc(o_step[z], 1)
        for j in range(4):
            dve.wait_ge(bank_free[j], phases[s][-1].use0[j] + 1)
        dve.wait_ge(mask_in, 16)

        def body(i):
            for z in range(2):
                h = 2 * i + z
                dve.wait_ge(o_done[z], i + 1)
                for d in range(DIRS):
                    V.tensor_tensor(hg_qp[z][:, d, :], hg_q[:, h, :], hg_f[d][:, h, :], ALU.mult).then_inc(q_step[z], 1)
            for lv in range(LEVELS):
                for z in range(2):
                    h = 2 * i + z
                    dve.wait_ge(scr_done[z], SCORE_STEPS * i + 2 + lv)
                    dve.wait_ge(q_step[z], Q_STEPS * i + Q_AT[lv] + 1)
                    if lv > 0:
                        dve.wait_ge(t_step[z], T_STEPS * i + 1 + lv)
                    for d in range(DIRS):
                        if lv == 0 and d == 0:
                            dve.wait_ge(diag_copied[z], i + 1)
                        elif d == 1 and lv < LOW:
                            dve.wait_ge(q_step[z], Q_STEPS * i + Q_AT[lv] + 2 + 1)
                        part = halves(hg_qp[z][:, d, :], 1 << lv)[:, :, 1 - d]
                        V.tensor_tensor(part, part, decay(z, d, h, lv, d), ALU.mult).then_inc(q_step[z], 1)
                        if lv < LOW:
                            mask = hg_mask[:, d, lv, :].bitcast(I32).unsqueeze(1).to_broadcast([P, NT, 32])
                            low = psum[SCORE + z][:, d * NT * 32:(d + 1) * NT * 32].rearrange("p (t q) -> p t q", t=NT)
                            V.copy_predicated(hg_low[z][:, :, :], mask, low).then_inc(q_step[z], 1)
            for z in range(2):
                dve.wait_ge(kr_turned[z], i + 2)
                dve.wait_ge(t_step[z], T_STEPS * (i + 1))
                dve.wait_ge(q_step[z], Q_STEPS * i + Q_AT[LEVELS] + 1)
                for d in range(DIRS):
                    far = hg_qp[z][:, d, (2 - d) * P:(3 - d) * P]
                    at = DECAYS[LEVELS - 1] + 1 + d
                    V.tensor_scalar(far, far, hg_t[z][:, d, at:at + 1], None, ALU.mult).then_inc(q_step[z], 1)
            for z in range(2):
                dve.wait_ge(o_var[z], i + 1)
                V.tensor_scalar(hg_r[z][:, :], psum[HIGH + z][:, 0:T], 1.0 / P, EPS, ALU.mult,
                                ALU.add).then_inc(var_read[z], 1)
            for z in range(2):
                h = 2 * i + z
                dve.wait_ge(root_made[z], i + 1)
                V.tensor_tensor(tmp[:, z, :], psum[OUT + z][:, 0:T], hg_r[z][:, :], ALU.mult).then_inc(o_step[z], 1)
                dve.wait_ge(o_step[z], 2 * i + 2)
                dve.wait_ge(o_lo_made, DC * mi + h - 1 + CREDIT)
                for dst, made in ((tmp[:, 2 + z, :], o_step[z]), (o_hi[:, h, :], mix_hi_made)):
                    V.scalar_tensor_tensor(out=dst, in0=tmp[:, z, :], scalar=misc[:, NG:NG + 1],
                                           in1=hg_g[:, h, :], op0=ALU.mult, op1=ALU.mult).then_inc(made, 1)
        loop(dve, PAIRS, body)

    def gp_hgrn_core(gp, s):
        G = nc.gpsimd
        mi = mixer_number(s)
        half_b = m_half[:, 0:1].to_broadcast([P, T])

        def body(i):
            for z in range(2):
                gp.wait_ge(k_init[z], 2 * i + 2)
                G.tensor_tensor(hg_ks[z][:, :], hg_kr[z][:, 0, :], hg_kr[z][:, 1, :], ALU.add).then_inc(k_step[z], 1)
            for lv in range(LEVELS):
                for z in range(2):
                    if lv == 0:
                        gp.wait_ge(q_step[z], Q_STEPS * i + 1)
                    gp.wait_ge(scr_done[z], SCORE_STEPS * i + 2 + lv)
                    gp.wait_ge(k_step[z], K_STEPS * i + 1 + 2 * lv)
                    h = 2 * i + z
                    if lv == 0:
                        for d in range(DIRS):
                            f = hg_f[d][:, h, :].rearrange("p (n two) -> p n two", two=2)
                            G.tensor_tensor(hg_t[z][:, d, 0:DECAYS[1]], f[:, :, 0], f[:, :, 1],
                                            ALU.mult).then_inc(t_step[z], 1)
                    else:
                        gp.wait_ge(t_step[z], T_STEPS * i + 1 + lv)
                        t = hg_t[z][:, :, DECAYS[lv - 1]:DECAYS[lv]].rearrange("p d (n two) -> p d n two", two=2)
                        G.tensor_tensor(hg_t[z][:, :, DECAYS[lv]:DECAYS[lv + 1]], t[:, :, :, 0], t[:, :, :, 1],
                                        ALU.mult).then_inc(t_step[z], 1)
                    for d in range(DIRS):
                        part = halves(hg_kr[z][:, d, :], 1 << lv)[:, :, d]
                        G.tensor_tensor(part, part, decay(z, d, h, lv, 1 - d), ALU.mult).then_inc(k_step[z], 1)
            for z in range(2):
                gp.wait_ge(var_read[z], i + 2)
                G.tensor_tensor(hg_r[z][:, :], hg_r[z][:, :], half_b, ALU.pow).then_inc(root_made[z], 1)
            for z in range(2):
                gp.wait_ge(mix_hi_made, DC * mi + 2 * i + z + 1)
                h = 2 * i + z
                G.tensor_tensor(o_lo[:, h, :], tmp[:, 2 + z, :], o_hi[:, h, :].bitcast(F32),
                                ALU.subtract).then_inc(o_lo_made, 1)
        loop(gp, PAIRS, body)

    block_ctx = nc.Block()
    blk = block_ctx.__enter__()

    @blk.sync
    def _(sp):
        def load_block(ph, i, j):
            b = ph.block0 + 4 * i + j
            sp.wait_ge(w_lo_made, b - 3 + CREDIT)
            dst = raw[:, j, 0:ph.tiles * P].rearrange("p (k n) -> p k n", n=P)
            sp.dma_start(dst, ph.src(i, j)).then_inc(raw_landed[j], 16)

        ADA_PER_LAYER = N_MOD * D // ADA_COLS

        def load_ada(n, first=False):
            for h in range(2):
                if not first:
                    sp.wait_ge(ada_used[h], n)
                sp.dma_start(ada_raw[:, h, :, :], ada_src(n, h)).then_inc(ada_landed[h], 16)

        def ada_src(n, h):
            layer = ada_layer[0]
            col = (n - layer * ADA_PER_LAYER) * ADA_COLS
            v = W["w_ada"][layer, h * (D // 2):(h + 1) * (D // 2), :].rearrange("(k p) n -> p k n", p=P)
            return v[:, :, bass.ds(col, ADA_COLS)]

        ada_layer = [0]

        def run_phase(ph):
            skip = 1 if ph is flat[0] or ph.kind == "mix_out" else 0

            def body_at(lo, hi, ada_on, layer):
                ada_layer[0] = layer

                def body(i0):
                    i = i0 + lo
                    for j in range(4):
                        load_block(ph, i, j)
                    if ada_on:
                        load_ada(ph.ada0 + i)
                loop(sp, hi - lo, body)
            if not ph.ada:
                body_at(skip, ph.groups, False, 0)
                return
            if skip:
                load_ada(ph.ada0)
            cut = skip
            while cut < ph.groups:
                layer = (ph.ada0 + cut) // ADA_PER_LAYER
                stop = min(ph.groups, (layer + 1) * ADA_PER_LAYER - ph.ada0)
                body_at(cut, stop, True, layer)
                cut = stop

        sp.dma_start(base_k[:, :], ins["k_base"]).then_inc(consts_in, 16)
        bias_rows = W["b_ada"].rearrange("l (r p) -> (l r) p", p=P)
        gain_rows = W["norm_g"].rearrange("l n (r p) -> (l n r) p", p=P)
        for n, (src, r0, nr) in enumerate(((bias_rows, 0, 128), (bias_rows, 128, 128), (bias_rows, 256, 32),
                                           (gain_rows, 0, 128), (gain_rows, 128, 64))):
            sp.dma_start(vin[0:nr, n, :], src[r0:r0 + nr, :]).then_inc(vec_in, 16)
        for r0, nr, src in ((CW, 24, W["conv_w"].rearrange("l j (r p) -> (l j r) p", p=P)),
                            (CB, 8, W["conv_b"].rearrange("l (r p) -> (l r) p", p=P)),
                            (CC, 8, W["c"].rearrange("b (r p) -> (b r) p", p=P)),
                            (CX, 8, W["c_ctx"].rearrange("(r p) -> r p", p=P)),
                            (LB, 64, W["hgrn_lb"].rearrange("d l (r p) -> (d l r) p", p=P)),
                            (NG, 1, W["hgrn_norm_g"])):
            sp.dma_start(vin[r0:r0 + nr, 5, :], src).then_inc(vec_in, 16)
        load_ada(0, first=True)
        sp.dma_start(xin[:, 0, :], W["x_prompt"][0]).then_inc(x_in, 16)
        sp.dma_start(xin[:, 1:3, :], W["x_sample"][0].rearrange("(t p) d -> p t d", p=P)).then_inc(x_in, 16)
        for n in range(1, ADA_FIRST):
            load_ada(n)
            if n == 1:
                for j in range(4):
                    load_block(flat[0], 0, j)
        for s in range(N_SUB):
            for n, ph in enumerate(phases[s]):
                if ph.kind == "mix_out":
                    for j in range(4):
                        load_block(ph, 0, j)
                    sp_core(sp, s, load_ada, ada_layer)
                run_phase(ph)
                if n == 0:
                    sp_core_start(sp, s)
        sp.wait_ge(turn_copied_a, TURN_A_END)
        sp.wait_ge(turn_copied_v, TURN_V_END)
        sp.dma_start(outs["y_prompt"][0], yout[:, 0, :]).then_inc(out_stored, 16)
        sp.dma_start(outs["y_sample"][0].rearrange("(t p) d -> p t d", p=P), yout[:, 1:3, :]).then_inc(out_stored, 16)
        sp.wait_ge(out_stored, 16 * (2 + stores_until(N_SUB)))
        if "hgrn" in sub_kind:
            for z in range(2):
                sp.wait_ge(state_stored[z], 16 * (PAIRS + 1))

    @blk.tensor
    def _(pe):
        mm = nc.tensor.matmul

        def block_products(ph, i, j):
            b = ph.block0 + 4 * i + j
            hi, lo = moving_of[ph.moving]
            halves = ph.kind == "ffn_out"
            opens, closes = (j % 2 == 0, j % 2 == 1) if halves else (True, True)
            bank = j - j % 2 if halves else j
            first_tile = HT * (j % 2) if halves else 0
            pe.wait_ge(w_lo_made, b + 1 + CREDIT)
            if opens and ph.kind in OUT_KINDS:
                pe.wait_ge(bank_free[bank], ph.use0[bank] + 1)
                pe.wait_ge(sq_out_made, DC * ph.s + (2 * i + j // 2 - 1 if halves else 4 * i + j - 3) + CREDIT)
            elif opens:
                pe.wait_ge(bank_free[bank], ph.use0[bank] + i + 1)
            if halves and j < 2:
                pe.wait_ge(h2_lo_made, h2_base(ph.s) + HT * (j + 1) + 2)
            for k in range(ph.tiles):
                if ph.moving == "h" and j == 0 and ph is phases[ph.s][0]:
                    pe.wait_ge(h_lo_made, DC * ph.s + k + 1)
                if ph.moving == "o" and j == 0:
                    pe.wait_ge(o_lo_made, DC * mixer_number(ph.s) + k + 1 + CREDIT)
                wh = w_hi[:, j, k * P:(k + 1) * P]
                wl = w_lo[:, j, k * P:(k + 1) * P]
                out = psum[bank][:, 0:T]
                mm(out, wh, hi[:, first_tile + k, :], start=(opens and k == 0), stop=False)
                mm(out, wh, lo[:, first_tile + k, :], start=False, stop=False)
                last = mm(out, wl, hi[:, first_tile + k, :], start=False, stop=(closes and k == ph.tiles - 1))
            last.then_inc(block_done, 1)

        def ada_products(n, first=False):
            for h in range(2):
                pe.wait_ge(ada_landed[h], 16 * (n + 1))
                if h == 0 and not first:
                    pe.wait_ge(ada_copied, n)
                for g in range(4):
                    last = mm(psum[ADA_ACC][32 * g:32 * g + 32, 0:ADA_COLS], cond[:, 4 * h + g, :],
                              ada_raw[:, h, g, :], start=(h == 0), stop=(h == 1), tile_position=(0, 32 * g))
                last.then_inc(ada_used[h], 1)

        def ada_turn(n, first=False):
            pe.wait_ge(ada_copied, n + 1)
            if not first:
                pe.wait_ge(mods_made, n)
            for c in range(2):
                last = mm(psum[ADA_T][:, 2 * c:2 * c + 2], ada_rows[:, c * P:(c + 1) * P], sel,
                          start=True, stop=True)
            last.then_inc(ada_turned, 1)

        def run_phase(ph):
            def body(i):
                if ph.ada:
                    ada_products(ph.ada0 + i)
                block_products(ph, i, 0)
                block_products(ph, i, 1)
                if ph.ada:
                    ada_turn(ph.ada0 + i)
                block_products(ph, i, 2)
                block_products(ph, i, 3)
            loop(pe, ph.groups, body)

        def stats(source, n):
            for t in range(NT):
                last = mm(psum[STAT][:, t:t + 1], source[:, t * P:(t + 1) * P], one_k, start=True, stop=True)
            last.then_inc(stat_done, 1)

        def spread(n):
            pe.wait_ge(diag_made, n + 1)
            mm(psum[SPREAD][:, 0:T], ones[:, :], diag[:, :, :].rearrange("p t q -> p (t q)"),
               start=True, stop=True).then_inc(spread_done, 1)

        def boundary(s):
            if s > 0:
                pe.wait_ge(acc_made, DC * s + 2)
                stats(acc, 2 * s - 1)
                spread(2 * s - 1)
            if s == N_SUB:
                return
            for c in range(DC):
                pe.wait_ge(y_sq_made, DC * s + c + 1)
                for t in range(NT):
                    last = mm(psum[STAT][:, 4 + t:5 + t], sq[:, c % 2, t * P:(t + 1) * P], one_k,
                              start=(c == 0 and t == 0), stop=(c == DC - 1), skip_group_check=True)
                last.then_inc(y_sq_used, 1)
            spread(2 * s)

        def turn(n, source, rows):
            bank = n % 4
            if n >= 4:
                pe.wait_ge(turn_copied_v if n % 2 == 0 else turn_copied_a, (n - 4) // 2 + 1)
            for q, src in enumerate(source):
                last = nc.tensor.transpose(psum[bank][:, q * P:q * P + rows], src, base_k[0:rows, 0:rows])
            last.then_inc(turn_done, 1)

        pe.sem_inc(block_done, CREDIT)
        pe.wait_ge(consts_in, 16)
        pe.wait_ge(vec_in, 16 * 11)
        for n, rows in enumerate(VEC_ROWS):
            turn(n, [vin[0:rows, n, :]], rows)
        pe.wait_ge(x_in, 32)
        for c in range(DC):
            turn(6 + c, [xin[:, t, c * P:(c + 1) * P] for t in range(NT)], P)
        pe.wait_ge(cond_made, 3)
        pe.wait_ge(consts_set, 3)
        for n in range(ADA_FIRST):
            ada_products(n, first=(n == 0))
            ada_turn(n, first=(n == 0))
        for s in range(N_SUB):
            boundary(s)
            for ph in phases[s]:
                if ph.kind == "mix_out":
                    pe_core(pe, s, ada_products, ada_turn)
                run_phase(ph)
        boundary(N_SUB)
        pe.wait_ge(y_made_v, 4 * N_SUB)
        pe.wait_ge(y_made_p, 4 * N_SUB)
        for n in range(TURNS_END):
            t, half = n // 2, n % 2
            turn(TURNS_START + n, [y[:, 4 * half + q, t * P:(t + 1) * P] for q in range(4)], P)

    @blk.scalar
    def _(act):
        A = nc.scalar.activation

        def split(ph, i, j):
            b = ph.block0 + 4 * i + j
            act.wait_ge(raw_landed[j], 16 * (ph.block0 // 4 + i + 1))
            act.wait_ge(block_done, b - 3 + CREDIT)
            n = ph.tiles * P
            A(w_hi[:, j, 0:n], raw[:, j, 0:n], ACT.Copy).then_inc(w_hi_made, 1)

        def split_next(ph):
            nxt = following[id(ph)]
            if nxt is not None:
                split(nxt, 0, 0)
                split(nxt, 0, 1)

        def ada_copy(n, first=False):
            act.wait_ge(ada_used[1], n + 1)
            if not first:
                act.wait_ge(ada_turned, n)
            A(ada_rows[:, :], psum[ADA_ACC][:, 0:ADA_COLS], ACT.Copy).then_inc(ada_copied, 1)

        def out_tile(ph, m, bank, block):
            act.wait_ge(block_done, block + 1 + CREDIT)
            act.wait_ge(acc_made, DC * ph.s + m + 1)
            for g, (a, b) in enumerate(GROUPS):
                A(og[:, m, a:b], psum[bank][:, a:b], ACT.Identity, scale=g_out[:, m, g:g + 1])
            A(sq[:, bank // 2 % 2 if ph.kind == "ffn_out" else bank % 2, :], psum[bank][:, 0:T],
              ACT.Square).then_inc(sq_out_made, 1)

        def evac(ph, i, half):
            ja, jb = 2 * half, 2 * half + 1
            block = ph.block0 + 4 * i
            if ph.kind == "ffn_in":
                act.wait_ge(block_done, block + ja + 1 + CREDIT)
                act.wait_ge(bank_free[jb], ph.use0[jb] + i + 1)
                A(tmp[:, half, :], psum[ja][:, 0:T], ACT.Silu).then_inc(bank_free[ja], 1)
            elif ph.kind == "ffn_out":
                if half == 0:
                    act.wait_ge(g_ready, ph.s + 1)
                out_tile(ph, 2 * i + half, ja, block + jb)
            elif ph.kind == "mix_out":
                if half == 0:
                    act.wait_ge(g_ready, ph.s + 1)
                for j in (ja, jb):
                    out_tile(ph, 4 * i + j, j, block + j)
            else:
                act_mix(act, ph, i, half)

        def run_phase(ph):
            def body(i):
                split(ph, i, 2)
                split(ph, i, 3)
                if ph.ada:
                    ada_copy(ph.ada0 + i)
                evac(ph, i, 0)
                split(ph, i + 1, 0)
                split(ph, i + 1, 1)
                evac(ph, i, 1)
            i = ph.groups - 1
            loop(act, i, body)
            split(ph, i, 2)
            split(ph, i, 3)
            if ph.ada:
                ada_copy(ph.ada0 + i)
            evac(ph, i, 0)
            split_next(ph)
            evac(ph, i, 1)

        def boundary(s):
            for c in range(DC):
                if s == 0:
                    act.wait_ge(turn_copied_v if c % 2 == 0 else turn_copied_a, (6 + c) // 2 + 1)
                else:
                    act.wait_ge(y_made_v if c % 2 == 0 else y_made_p, 4 * (s - 1) + c // 2 + 1)
                if c >= 2:
                    act.wait_ge(y_sq_used, DC * s + c - 1)
                A(sq[:, c % 2, :], y[:, c, :], ACT.Square).then_inc(y_sq_made, 1)
            act.wait_ge(s_ready, s + 1)
            for c in range(DC):
                act.wait_ge(u_made, DC * s + c + 1)
                if c >= 2:
                    act.wait_ge(h_lo_made, DC * s + c - 1)
                for g, (a, b) in enumerate(GROUPS):
                    last = A(tmp[:, 2 + c % 2, a:b], tmp[:, c % 2, a:b], ACT.Identity,
                             bias=mod[:, mod_col(s, 0) + c, g:g + 1], scale=s_cols[:, c, g:g + 1])
                last.then_inc(hm_made, 1)

        def turn_copy(n, dst, src):
            act.wait_ge(turn_done, n + 1)
            A(dst, src, ACT.Copy).then_inc(turn_copied_a, 1)

        act.sem_inc(sq_out_made, CREDIT)
        for n, dst in ((1, b_cols[:, 128:256]), (3, g_cols[:, 0:128]), (5, misc[:, :])):
            turn_copy(n, dst, psum[n % 4][:, 0:VEC_ROWS[n]])
        act.wait_ge(turn_copied_a, 3)
        act.wait_ge(cond_made, 1)
        A(cond[:, :, 0], misc[:, CX:CX + DC], ACT.Silu).then_inc(cond_made, 1)
        A(cond[:, :, 1], misc[:, CC:CC + DC], ACT.Silu).then_inc(cond_made, 1)
        for c in range(1, DC, 2):
            turn_copy(6 + c, y[:, c, :], psum[(6 + c) % 4][:, 0:T])
        split(flat[0], 0, 0)
        split(flat[0], 0, 1)
        for n in range(ADA_FIRST):
            ada_copy(n, first=(n == 0))
        for s in range(N_SUB):
            boundary(s)
            for ph in phases[s]:
                if ph.kind == "hgrn_q":
                    act_lower_bound(act)
                if ph.kind == "mix_out":
                    act_core(act, s, ada_copy)
                run_phase(ph)
        for n in range(1, TURNS_END, 2):
            turn_copy(TURNS_START + n, yout[:, n // 2, 512:1024], psum[(TURNS_START + n) % 4][:, :])

    @blk.vector
    def _(dve):
        V = nc.vector

        def split(ph, i, j):
            b = ph.block0 + 4 * i + j
            dve.wait_ge(w_hi_made, b + 1)
            n = ph.tiles * P
            V.tensor_tensor(w_lo[:, j, 0:n], raw[:, j, 0:n], w_hi[:, j, 0:n].bitcast(F32),
                            ALU.subtract).then_inc(w_lo_made, 1)

        def split_next(ph):
            nxt = following[id(ph)]
            if nxt is not None:
                split(nxt, 0, 0)
                split(nxt, 0, 1)

        def mod_add(n):
            dve.wait_ge(ada_turned, n + 1)
            bias = b_cols[:, bass.ds(2 * n, 2)].unsqueeze(2).to_broadcast([P, 2, 2])
            V.tensor_tensor(mod[:, bass.ds(2 * n, 2), :], psum[ADA_T][:, 0:4].rearrange("p (c g) -> p c g", g=2),
                            bias, ALU.add).then_inc(mods_made, 1)

        def evac(ph, i, half):
            ja, jb = 2 * half, 2 * half + 1
            block = ph.block0 + 4 * i
            if ph.kind == "ffn_in":
                pair = 2 * i + half
                dve.wait_ge(bank_free[ja], ph.use0[ja] + i + 2)
                dve.wait_ge(block_done, block + jb + 1 + CREDIT)
                dve.wait_ge(h2_lo_made, h2_base(ph.s) + pair + 1)
                V.tensor_tensor(tmp[:, 2 + half, :], psum[jb][:, 0:T], tmp[:, half, :],
                                ALU.mult).then_inc(bank_free[jb], 1)
                dve.wait_ge(bank_free[jb], ph.use0[jb] + i + 2)
                V.tensor_copy(h2_hi[:, pair, :], tmp[:, 2 + half, :]).then_inc(h2_hi_made, 1)
            elif ph.kind not in OUT_KINDS:
                dve_mix(dve, ph, i, half)

        def run_phase(ph):
            def body(i):
                split(ph, i, 2)
                split(ph, i, 3)
                evac(ph, i, 0)
                if ph.ada:
                    mod_add(ph.ada0 + i)
                split(ph, i + 1, 0)
                split(ph, i + 1, 1)
                evac(ph, i, 1)
            i = ph.groups - 1
            loop(dve, i, body)
            split(ph, i, 2)
            split(ph, i, 3)
            evac(ph, i, 0)
            if ph.ada:
                mod_add(ph.ada0 + i)
            split_next(ph)
            evac(ph, i, 1)

        def rms(n, cols):
            V.tensor_scalar(r_var, cols, EPS, None, ALU.add).then_inc(var_made, 1)
            dve.wait_ge(std_made, n + 1)
            V.tensor_tensor(diag[:, :, :], ident.unsqueeze(1).to_broadcast([P, NT, P]),
                            r_std.unsqueeze(2).to_broadcast([P, NT, P]), ALU.mult).then_inc(diag_made, 1)

        def boundary(s):
            if s > 0:
                dve.wait_ge(stat_done, s)
                rms(2 * s - 1, psum[STAT][:, 0:NT])
                dve.wait_ge(spread_done, 2 * s)

                def scaled(c):
                    if c >= 4:
                        dve.wait_ge(y_made_v if c % 2 == 0 else y_made_p, 4 * (s - 1) + c // 2 - 1)
                    V.tensor_tensor(tmp[:, c % 4, :], og[:, c, :], psum[SPREAD][:, 0:T],
                                    ALU.mult).then_inc(t_made, 1)

                scaled(0)
                scaled(1)
                for c in range(0, DC, 2):
                    if c + 2 < DC:
                        scaled(c + 2)
                    dve.wait_ge(t_made, DC * (s - 1) + c + 1)
                    V.tensor_tensor(y[:, c, :], y[:, c, :], tmp[:, c % 4, :], ALU.add).then_inc(y_made_v, 1)
                    if c + 3 < DC:
                        scaled(c + 3)
            if s == N_SUB:
                return
            dve.wait_ge(y_sq_used, DC * (s + 1))
            rms(2 * s, psum[STAT][:, 4:4 + NT])
            dve.wait_ge(spread_done, 2 * s + 1)

            def normed(c):
                if c >= 2:
                    dve.wait_ge(hm_made, DC * s + c - 1)
                V.tensor_tensor(tmp[:, c % 2, :], y[:, c, :], psum[SPREAD][:, 0:T], ALU.mult).then_inc(u_made, 1)

            normed(0)
            for c in range(DC):
                if c + 1 < DC:
                    normed(c + 1)
                dve.wait_ge(hm_made, DC * s + c + 1)
                V.tensor_copy(h_hi[:, c, :], tmp[:, 2 + c % 2, :]).then_inc(h_hi_made, 1)

        def turn_copy(n, dst, src):
            dve.wait_ge(turn_done, n + 1)
            V.tensor_copy(dst, src).then_inc(turn_copied_v, 1)

        V.memset(cond[:, :, :], 0.0).then_inc(cond_made, 1)
        V.memset(ones[:, :], 1.0).then_inc(consts_set, 1)
        V.memset(m_half, -0.5).then_inc(consts_set, 1)
        V.memset(one_k, 1.0 / D).then_inc(consts_set, 1)
        for x in range(4):
            dve.sem_inc(bank_free[x], 1)
        dve.sem_inc(w_lo_made, CREDIT)
        for n, dst in ((0, b_cols[:, 0:128]), (2, b_cols[:, 256:288]), (4, g_cols[:, 128:192])):
            turn_copy(n, dst, psum[n % 4][:, 0:VEC_ROWS[n]])
        for c in range(0, DC, 2):
            turn_copy(6 + c, y[:, c, :], psum[(6 + c) % 4][:, 0:T])
        split(flat[0], 0, 0)
        split(flat[0], 0, 1)
        dve.wait_ge(turn_copied_v, 2)
        dve.wait_ge(turn_copied_a, 1)
        for n in range(ADA_FIRST):
            mod_add(n)
        for s in range(N_SUB):
            boundary(s)
            for ph in phases[s]:
                if ph.kind == "hgrn_q":
                    dve_lower_bound(dve)
                if ph.kind == "mix_out":
                    dve_core(dve, s, mod_add)
                run_phase(ph)
        boundary(N_SUB)
        for n in range(0, TURNS_END, 2):
            turn_copy(TURNS_START + n, yout[:, n // 2, 0:512], psum[(TURNS_START + n) % 4][:, :])

    @blk.gpsimd
    def _(gp):
        G = nc.gpsimd

        def gains(s, post):
            which = 2 if post else 1
            gp.wait_ge(mods_made, mods_needed(s, which))
            g = g_cols[:, norm_col(s, post):norm_col(s, post) + DC].unsqueeze(2).to_broadcast([P, DC, 2])
            dst = (g_out if post else s_cols)[:, :, :]
            ready = g_ready if post else s_ready
            m = mod[:, mod_col(s, which):mod_col(s, which) + DC, :]
            mixer = s % 3 == 1
            if post and mixer:
                G.tensor_tensor(dst, m, g, ALU.mult).then_inc(ready, 1)
                return
            n = cols_n[0] = cols_n[0] + 1
            G.tensor_tensor(dst, m, g, ALU.mult).then_inc(cols_step, 1)
            gp.wait_ge(cols_step, n)
            if post:
                G.tensor_scalar(dst, dst, 0.5, None, ALU.mult).then_inc(ready, 1)
            else:
                G.tensor_tensor(dst, dst, g, ALU.add).then_inc(ready, 1)

        cols_n = [0]

        def root(n):
            gp.wait_ge(var_made, n + 1)
            G.tensor_tensor(r_std, r_var, m_half, ALU.pow).then_inc(std_made, 1)

        def boundary(s):
            if s > 0:
                root(2 * s - 1)
                for c in range(1, DC, 2):
                    gp.wait_ge(t_made, DC * (s - 1) + c + 1)
                    G.tensor_tensor(y[:, c, :], y[:, c, :], tmp[:, c % 4, :], ALU.add).then_inc(y_made_p, 1)
            if s == N_SUB:
                return
            root(2 * s)
            for c in range(DC):
                gp.wait_ge(h_hi_made, DC * s + c + 1)
                G.tensor_tensor(h_lo[:, c, :], tmp[:, 2 + c % 2, :], h_hi[:, c, :].bitcast(F32),
                                ALU.subtract).then_inc(h_lo_made, 1)
            G.memset(acc[:, :], 0.0).then_inc(acc_zeroed, 1)

        def add_squares(ph, m, place):
            gp.wait_ge(sq_out_made, DC * ph.s + m + 1 + CREDIT)
            gp.wait_ge(acc_made, DC * ph.s + m + 2)
            G.tensor_tensor(acc[:, :], acc[:, :], sq[:, place, :], ALU.add).then_inc(acc_made, 1)

        def run_phase(ph):
            def body(i):
                if ph.kind == "ffn_in":
                    for half in range(2):
                        pair = 2 * i + half
                        gp.wait_ge(h2_hi_made, h2_base(ph.s) + pair + 1)
                        G.tensor_tensor(h2_lo[:, pair, :], tmp[:, 2 + half, :], h2_hi[:, pair, :].bitcast(F32),
                                        ALU.subtract).then_inc(h2_lo_made, 1)
                elif ph.kind == "ffn_out":
                    for half in range(2):
                        add_squares(ph, 2 * i + half, half)
                elif ph.kind == "mix_out":
                    for j in range(4):
                        add_squares(ph, 4 * i + j, j % 2)
                else:
                    gp_mix(gp, ph, i)
            if ph.kind in OUT_KINDS:
                gains(ph.s, 1)
                gp.wait_ge(acc_zeroed, ph.s + 1)
            loop(gp, ph.groups, body)

        gp.sem_inc(h2_lo_made, 2)
        gp.sem_inc(acc_made, 2)
        gp.sem_inc(o_lo_made, CREDIT)
        gp.wait_ge(turn_copied_a, 2)
        gp.wait_ge(turn_copied_v, 3)
        gp.wait_ge(consts_set, 3)
        for s in range(N_SUB):
            gains(s, 0)
            boundary(s)
            for ph in phases[s]:
                if ph.kind == "mix_out":
                    gp_core(gp, s)
                run_phase(ph)
        boundary(N_SUB)

    block_ctx.__exit__(None, None, None)
    sem_stack.close()
    psum_stack.close()


INPUTS = ["x_prompt", "x_sample", "cache_k", "cache_v", "state_hgrn", "c", "c_ctx", "w_ada", "b_ada", "norm_g",
          "w_ffn_in", "w_ffn_out", "w_attn_qkv", "w_attn_o", "attn_sink", "w_conv_in", "conv_w", "conv_b",
          "w_conv_out", "w_hgrn_in", "hgrn_lb", "hgrn_norm_g", "w_hgrn_out"]
OUTPUTS = [("y_prompt", (1, TP, D)), ("y_sample", (1, TS, D)), ("new_k", (1, 2, TP, KVH, HD)),
           ("new_v", (1, 2, TP, KVH, HD)), ("new_state", (1, 1, 2, HG, P, P))]


def kernel(**inputs):
    import concourse.bacc as bacc
    from concourse.bass_utils import run_bass_kernel_spmd

    nc = bacc.Bacc("TRN2", target_bir_lowering=False, num_devices=1)
    arrays = {name: np.ascontiguousarray(inputs[name]) for name in INPUTS}
    arrays.update(host_constants())
    ins = {name: nc.dram_tensor(name, a.shape, mybir.dt.from_np(a.dtype), kind="ExternalInput").ap()
           for name, a in arrays.items()}
    outs = {name: nc.dram_tensor(name, shape, F32, kind="ExternalOutput").ap() for name, shape in OUTPUTS}
    build(nc, ins, outs)
    results = run_bass_kernel_spmd(nc, [arrays], core_ids=[0]).results[0]
    return tuple(results[name] for name, _ in OUTPUTS)
```
